# Optimizing a Trainium2 kernel written in Bass

```python
import jax, jax.numpy as jnp
from jax import lax
import numpy as np

D_MODEL = 1024
BATCH = 1
SEQ = 256
DEPTH = 1

CHUNK = 64
N_META = 16

POOL_WIDTH = 512
POOL_WINDOWS = (2, 4, 8, 16)
POOL_GROUPS = len(POOL_WINDOWS)
POOL_GROUP_DIM = POOL_WIDTH // POOL_GROUPS
POOL_OUT_DIM = D_MODEL // POOL_GROUPS

CONV_WIDTH = 512
CONV_KERNEL = 31

N_BRANCHES = 2
IN_COLS = POOL_WIDTH + 2 * CONV_WIDTH + N_BRANCHES * D_MODEL

N_EXPERTS = 32
TOP_K = 4
D_EXPERT = D_MODEL
SWIGLU_LIMIT = 7.0
SWIGLU_ALPHA = 1.702
MOE_BLOCK = 256

RMS_EPS = 1e-5
LN_EPS = 1e-5

kernel_name = "hybrid_pool_conformerconv_moe_block"

def rmsnorm(x, g):
    xf = x.astype(jnp.float32)
    y = xf * lax.rsqrt(jnp.mean(xf * xf, axis=-1, keepdims=True) + RMS_EPS)
    return (y * g.astype(jnp.float32)).astype(x.dtype)

def pool_mixer(u, w_grp, scale):
    b, l, _ = u.shape
    uf = u.astype(jnp.float32)
    cs = jnp.cumsum(uf, axis=1)
    t = jnp.arange(1, l + 1, dtype=jnp.float32)[None, :, None]
    outs = []
    for g, w in enumerate(POOL_WINDOWS):
        c = cs[..., g * POOL_GROUP_DIM:(g + 1) * POOL_GROUP_DIM]
        c_prev = jnp.pad(c, ((0, 0), (w, 0), (0, 0)))[:, :l]
        mean = (c - c_prev) / jnp.minimum(t, float(w))
        outs.append(mean - uf[..., g * POOL_GROUP_DIM:(g + 1) * POOL_GROUP_DIM])
    d = jnp.stack(outs, axis=2).astype(u.dtype)
    y = jnp.einsum('blgc,gcd->blgd', d, w_grp).reshape(b, l, D_MODEL)
    return y * scale

def conformer_conv(v, gt, k_dw, b_dw, ln_g, ln_b, w_pw2, b_pw2):
    a = v * jax.nn.sigmoid(gt)
    c = lax.conv_general_dilated(
        a, k_dw[:, None, :], window_strides=(1,),
        padding=[(CONV_KERNEL - 1, 0)],
        dimension_numbers=('NWC', 'WIO', 'NWC'),
        feature_group_count=CONV_WIDTH) + b_dw
    cf = c.astype(jnp.float32)
    mu = jnp.mean(cf, axis=-1, keepdims=True)
    var = jnp.mean(jnp.square(cf - mu), axis=-1, keepdims=True)
    cn = ((cf - mu) * lax.rsqrt(var + LN_EPS) * ln_g.astype(jnp.float32)
          + ln_b.astype(jnp.float32)).astype(v.dtype)
    return jax.nn.silu(cn) @ w_pw2 + b_pw2

def moe_ffn(h, router_w, router_b, w_gu, b_gu, w_dn, b_dn):
    n_tok = h.shape[0]
    logits = h.astype(jnp.float32) @ router_w.astype(jnp.float32) + router_b.astype(jnp.float32)
    top_v, top_i = lax.top_k(logits, TOP_K)
    gates = jax.nn.softmax(top_v, axis=-1)

    n_assign = n_tok * TOP_K
    e_flat = top_i.reshape(-1)
    tok_flat = jnp.arange(n_assign, dtype=jnp.int32) // TOP_K
    g_flat = gates.reshape(-1)
    order = jnp.argsort(e_flat)
    se, stok, sg = e_flat[order], tok_flat[order], g_flat[order]

    counts = jnp.bincount(e_flat, length=N_EXPERTS)
    padded = (counts + MOE_BLOCK - 1) // MOE_BLOCK * MOE_BLOCK
    start = jnp.cumsum(counts) - counts
    pend = jnp.cumsum(padded)
    pstart = pend - padded
    dest = pstart[se] + jnp.arange(n_assign, dtype=jnp.int32) - start[se]

    n_blocks = -(-n_assign // MOE_BLOCK) + N_EXPERTS
    n_slots = n_blocks * MOE_BLOCK
    slot_tok = jnp.zeros((n_slots,), jnp.int32).at[dest].set(stok)
    slot_g = jnp.zeros((n_slots,), jnp.float32).at[dest].set(sg)
    block_e = jnp.minimum(
        jnp.searchsorted(pend, jnp.arange(n_blocks, dtype=pend.dtype) * MOE_BLOCK, side='right'),
        N_EXPERTS - 1)

    def expert_block(args):
        idx, gw, e = args
        xb = h[idx]
        gu = xb @ w_gu[e] + b_gu[e]
        gate, up = gu[:, :D_EXPERT], gu[:, D_EXPERT:]
        gate = jnp.minimum(gate, SWIGLU_LIMIT)
        up = jnp.clip(up, -SWIGLU_LIMIT, SWIGLU_LIMIT)
        act = (up + 1.0) * (gate * jax.nn.sigmoid(gate * SWIGLU_ALPHA))
        y = act @ w_dn[e] + b_dn[e]
        return y * gw[:, None].astype(y.dtype)

    y = lax.map(expert_block, (slot_tok.reshape(n_blocks, MOE_BLOCK),
                               slot_g.reshape(n_blocks, MOE_BLOCK), block_e))
    return jax.ops.segment_sum(y.reshape(n_slots, D_MODEL), slot_tok, num_segments=n_tok)

def setup_inputs(seed: int = 0) -> dict:
    key = jax.random.key(seed)
    ks = jax.random.split(key, 24)
    f32 = jnp.float32
    n = lambda k, s, sc: jax.random.normal(k, s, f32) * sc
    L_ = DEPTH
    return {
        "x": n(ks[0], (BATCH, SEQ, D_MODEL), 1.0),
        "meta_tokens": n(ks[1], (N_META, D_MODEL), 1.0),
        "norm_mix_g": 1.0 + n(ks[2], (L_, D_MODEL), 0.05),
        "w_in": n(ks[3], (L_, D_MODEL, IN_COLS), D_MODEL ** -0.5),
        "b_in": n(ks[4], (L_, IN_COLS), 0.02),
        "w_pool_grp": n(ks[5], (L_, POOL_GROUPS, POOL_GROUP_DIM, POOL_OUT_DIM), POOL_GROUP_DIM ** -0.5),
        "pool_scale": 1.0 + n(ks[6], (L_, D_MODEL), 0.1),
        "w_dwconv": n(ks[7], (L_, CONV_KERNEL, CONV_WIDTH), CONV_KERNEL ** -0.5),
        "b_dwconv": n(ks[8], (L_, CONV_WIDTH), 0.02),
        "conv_ln_g": 1.0 + n(ks[9], (L_, CONV_WIDTH), 0.05),
        "conv_ln_b": n(ks[10], (L_, CONV_WIDTH), 0.02),
        "w_pw2": n(ks[11], (L_, CONV_WIDTH, D_MODEL), CONV_WIDTH ** -0.5),
        "b_pw2": n(ks[12], (L_, D_MODEL), 0.02),
        "w_out": n(ks[13], (L_, D_MODEL, D_MODEL), D_MODEL ** -0.5),
        "norm_ffn_g": 1.0 + n(ks[14], (L_, D_MODEL), 0.05),
        "router_w": n(ks[15], (L_, D_MODEL, N_EXPERTS), D_MODEL ** -0.5),
        "router_b": n(ks[16], (L_, N_EXPERTS), 0.01),
        "w_gate_up": n(ks[17], (L_, N_EXPERTS, D_MODEL, 2 * D_EXPERT), D_MODEL ** -0.5),
        "b_gate_up": n(ks[18], (L_, N_EXPERTS, 2 * D_EXPERT), 0.02),
        "w_down": n(ks[19], (L_, N_EXPERTS, D_EXPERT, D_MODEL), D_EXPERT ** -0.5),
        "b_down": n(ks[20], (L_, N_EXPERTS, D_MODEL), 0.02),
        "norm_final_g": 1.0 + n(ks[21], (D_MODEL,), 0.05),
    }

def reference(x, meta_tokens, norm_mix_g, w_in, b_in, w_pool_grp, pool_scale,
              w_dwconv, b_dwconv, conv_ln_g, conv_ln_b, w_pw2, b_pw2, w_out,
              norm_ffn_g, router_w, router_b, w_gate_up, b_gate_up, w_down, b_down,
              norm_final_g):
    bsz, seq, d = x.shape
    meta = jnp.broadcast_to(meta_tokens[None].astype(x.dtype), (bsz, N_META, d))
    h = jnp.concatenate([meta, x], axis=1)
    length = seq + N_META
    c0 = POOL_WIDTH
    c1 = c0 + CONV_WIDTH
    c2 = c1 + CONV_WIDTH
    c3 = c2 + D_MODEL
    for l in range(DEPTH):
        xn = rmsnorm(h, norm_mix_g[l])
        proj = xn @ w_in[l] + b_in[l]
        u = proj[..., :c0]
        v = proj[..., c0:c1]
        gt = proj[..., c1:c2]
        g_a = proj[..., c2:c3]
        g_b = proj[..., c3:]
        y_a = pool_mixer(u, w_pool_grp[l], pool_scale[l])
        y_b = conformer_conv(v, gt, w_dwconv[l], b_dwconv[l], conv_ln_g[l], conv_ln_b[l],
                             w_pw2[l], b_pw2[l])
        mixed = jax.nn.sigmoid(g_a) * y_a + jax.nn.sigmoid(g_b) * y_b
        h = h + mixed @ w_out[l]
        hn = rmsnorm(h, norm_ffn_g[l]).reshape(bsz * length, d)
        h = h + moe_ffn(hn, router_w[l], router_b[l], w_gate_up[l], b_gate_up[l],
                        w_down[l], b_down[l]).reshape(bsz, length, d)
    h = rmsnorm(h, norm_final_g)
    return h[:, N_META:]


_drawn_inputs = setup_inputs


def setup_inputs(seed=0):
    import zlib

    import numpy as np

    out = dict(_drawn_inputs(seed))
    spreads = {}
    factors = {'b_gate_up': 5.768, 'b_down': 6.568}
    for name, (base, spread) in spreads.items():
        noise = np.random.default_rng([zlib.crc32(name.encode()), seed]).standard_normal(out[name].shape)
        drawn = base * np.exp(spread * noise) if base else spread * noise
        out[name] = __import__('jax').numpy.asarray(drawn.astype(out[name].dtype))
    for name, factor in factors.items():
        out[name] = (out[name] * factor).astype(out[name].dtype)
    return out
```

```python
from contextlib import ExitStack

import concourse.bass as bass
from concourse import mybir

ALU = mybir.AluOpType
ACT = mybir.ActivationFunctionType
F32 = mybir.dt.float32
I32 = mybir.dt.int32
U32 = mybir.dt.uint32
AX_X = mybir.AxisListType.X

P = 128
RMS_EPS = 1e-5
LN_EPS = 1e-5
SWIGLU_LIMIT = 7.0
SWIGLU_ALPHA = 1.702
TOP_K = 4
POOL_WINDOWS = (2, 4, 8, 16)
SLOTS = 64


def block_kernel(nc, x, meta_tokens, norm_mix_g, w_in, b_in, w_pool_grp, pool_scale, w_dwconv, b_dwconv,
                 conv_ln_g, conv_ln_b, w_pw2, b_pw2, w_out, norm_ffn_g, router_w, router_b, w_gate_up,
                 b_gate_up, w_down, b_down, norm_final_g, out):
    SEQ, D = x.shape[1], x.shape[2]
    META = meta_tokens.shape[0]
    L = SEQ + META
    CW = w_dwconv.shape[2]
    TAPS = w_dwconv.shape[1]
    E = router_w.shape[2]
    F = w_down.shape[2]
    KC = D // P
    FC = F // P
    CC = CW // P
    TT = SEQ // P
    PAIRS = E // 2
    PAD = TAPS - 1 - META
    LP = L + PAD
    assert (KC, FC, CC, TT, E) == (8, 8, 4, 2, 32) and PAD >= 0

    with ExitStack() as ctx:
        def sb(name, shape, dt=F32):
            return ctx.enter_context(nc.sbuf_tensor(name, shape, dt))

        def sem(name):
            return ctx.enter_context(nc.semaphore(name))

        gu_ring = sb("gu_ring", [P, 16, 2 * F])
        dn_ring = sb("dn_ring", [P, 4, 2 * D])
        h = sb("h", [P, TT, D])
        hs = sb("hs", [P, TT, D])
        mix = sb("mix", [P, 8, 256])
        work = sb("work", [P, 2, 512])
        sig = sb("sig", [P, 512])
        acts = sb("acts", [P, 2, 512])
        pick = sb("pick", [P, TT, 2 * SLOTS])
        weigh = sb("weigh", [P, TT, 2, 2, SLOTS])
        spread = sb("spread", [P, 2, SEQ])
        par = sb("par", [P, 2, P])
        bias = sb("bias", [6, 2, 512])
        seg = sb("seg", [6, 6, SLOTS])
        ident = sb("ident", [P, P])
        iota = sb("iota", [P, 2 * SLOTS])
        ss = sb("ss", [P, 8])
        rstd = sb("rstd", [P, 8])
        top = sb("top", [P, TT, 8])
        topi = sb("topi", [P, TT, 8], U32)
        topf = sb("topf", [P, TT, 8])
        negmax = sb("negmax", [P, TT])
        esum = sb("esum", [P, TT])
        erec = sb("erec", [P, TT])
        gates = sb("gates", [P, TT, E])
        place = sb("place", [P, TT, E])
        most = sb("most", [1, 1])
        flag = sb("flag", [1, 1], I32)
        ps = ctx.enter_context(nc.psum_tensor("ps", [P, 8, 512], F32))

        weighf = weigh[:, :, :, :, :].rearrange("p a b c d -> p (a b c d)")
        ones = weighf[:, 0:P]
        earlier = weighf[:, P:2 * P]
        logits = weighf[:, 256:256 + TT * E].rearrange("p (t e) -> p t e", t=TT)
        expl = weighf[:, 320:320 + TT * E].rearrange("p (t e) -> p t e", t=TT)
        rb = weighf[:, 384:384 + E]

        xg = mix[:, 0:4, :].rearrange("p a b -> p (a b)").rearrange("p (c s) -> p c s", s=2 * SLOTS)
        actT = mix[:, 4:8, :].rearrange("p a b -> p (a b)").rearrange("p (i b s) -> p i b s", i=2, b=FC // 2)
        junk_ffn = work[:, :, :].rearrange("p a b -> p (a b)")
        dnf = dn_ring[:, :, :].rearrange("p a b -> p (a b)")
        cut = [0]

        def take(a, b):
            o = cut[0]
            cut[0] += a * b
            assert cut[0] <= 8 * D
            return dnf[:, o:o + a * b].rearrange("p (a b) -> p a b", b=b)

        xnT = take(KC, L)
        glu = take(CC, LP)
        uT = take(CC, L)
        wpool = take(CC, 256)
        conv = take(CC, SEQ)
        sumA = take(CC, L)
        sq = sumA[:, :, :].rearrange("p a b -> p (a b)")[:, 0:CC * SEQ].rearrange("p (a b) -> p a b", b=SEQ)
        cvsig = uT[:, :, :].rearrange("p a b -> p (a b)")[:, 0:CC * SEQ].rearrange("p (a b) -> p a b", b=SEQ)
        hT = xnT[:, :, 0:SEQ]
        rw = take(KC, E)
        chosen = take(TT * TOP_K, E).rearrange("p (t k) e -> p t k e", t=TT)
        lnr = spread[:, 0, :]
        workf = work[:, :, :].rearrange("p a b -> p (a b)")
        gtsig = workf[:, 0:3 * L].rearrange("p (a b) -> p a b", b=L)
        sumB = workf[:, 0:3 * L].rearrange("p (a b) -> p a b", b=L)
        gasig = acts[:, :, :].rearrange("p a b -> p (a b)").rearrange("p (a b) -> p a b", b=SEQ)
        stage = acts[:, 0, 0:2 * P].rearrange("p (a b) -> p a b", b=P)
        gbsig = hs[:, :, :].rearrange("p a b -> p (a b)").rearrange("p (a b) -> p a b", b=SEQ)
        mixf = mix[:, :, :].rearrange("p a b -> p (a b)")
        meta = mixf[0:META, 0:D]
        junk = mixf[:, D:2 * D]

        rows = {}
        n = 0
        for name, ap in (("b_in", b_in), ("b_dw", b_dwconv), ("ln_g", conv_ln_g), ("ln_b", conv_ln_b),
                         ("b_pw2", b_pw2), ("scale", pool_scale), ("g_mix", norm_mix_g), ("g_ffn", norm_ffn_g)):
            k = ap.shape[1] // P
            rows[name] = (n, k, ap)
            n += k
        assert n <= P and TAPS * CC <= P
        ON_ACT = ("b_in", "g_mix", "b_dw", "ln_g")
        ON_SP = ("ln_b", "b_pw2", "scale", "g_ffn")

        def col(name, m, k=1):
            o = rows[name][0] + m
            return par[:, 0, o:o + k]

        def tap(k, c):
            return par[:, 1, k * CC + c:k * CC + c + 1]

        def wide(ap, k, w):
            return ap.unsqueeze(2).to_broadcast([P, k, w])

        def bank(b, a, w):
            return ps[:, b, 0:a * w].rearrange("p (a w) -> p a w", w=w)

        BLOCKS = [("v", CW, 12), ("gt", 2 * CW, 14), ("u", 0, 0), ("gA", 3 * CW, 2), ("gA", 3 * CW + 512, 4),
                  ("gB", 3 * CW + D, 6), ("gB", 3 * CW + D + 512, 8)]

        def win_block(i):
            s = BLOCKS[i][2]
            return gu_ring[:, s:s + 2, :].rearrange("p a b -> p (a b)").rearrange("p (k n) -> p k n", n=512)

        pw2_sb = gu_ring[:, 10:12, :].rearrange("p a b -> p (a b)").rearrange("p (c n) -> p c n", n=D)
        wout_sb = gu_ring[:, 12:16, :].rearrange("p a b -> p (a b)").rearrange("p (c n) -> p c n", n=D)
        gfin = workf
        outb = gu_ring[:, 1:3, 0:D]
        junk2 = gu_ring[:, 3, 0:D]

        x_in = [sem(f"x_in{t}") for t in range(TT)]
        meta_in = sem("meta_in")
        stage_clear = sem("stage_clear")
        stage_in = sem("stage_in")
        wpool_in = sem("wpool_in")
        router_in = sem("router_in")
        win_in = [sem(f"win_in{i}") for i in range(8)]
        pw2_in = sem("pw2_in")
        wout_in = sem("wout_in")
        consts_a = sem("consts_a")
        consts_made = sem("consts_made")
        squared = sem("squared")
        meaned = sem("meaned")
        rooted = sem("rooted")
        inverted = sem("inverted")
        scaled = sem("scaled")
        x_turned = sem("x_turned")
        par_turned = sem("par_turned")
        par_ready = sem("par_ready")
        xnT_ready = sem("xnT_ready")
        pads_made = sem("pads_made")
        proj_done = sem("proj_done")
        proj_read = sem("proj_read")
        glu_ready = sem("glu_ready")
        conv_step = sem("conv_step")
        pool_step = sem("pool_step")
        pooled = sem("pooled")
        pool_done = sem("pool_done")
        ya_ready = sem("ya_ready")
        ya_gated = sem("ya_gated")
        ln_summed = sem("ln_summed")
        centred = sem("centred")
        ln_squared = sem("ln_squared")
        var_summed = sem("var_summed")
        var_ready = sem("var_ready")
        dev_ready = sem("dev_ready")
        lnr_ready = sem("lnr_ready")
        normed = sem("normed")
        affine_done = sem("affine_done")
        cvsig_ready = sem("cvsig_ready")
        silu_ready = sem("silu_ready")
        pw2_done = sem("pw2_done")
        yb_gated = sem("yb_gated")
        mix_ready = sem("mix_ready")
        wout_done = sem("wout_done")
        hs_turned = sem("hs_turned")
        hT_ready = sem("hT_ready")
        logits_done = sem("logits_done")
        logits_ready = sem("logits_ready")
        top_ready = sem("top_ready")
        topi_ready = sem("topi_ready")
        topf_ready = sem("topf_ready")
        negmax_ready = sem("negmax_ready")
        exp_ready = sem("exp_ready")
        chosen_step = sem("chosen_step")
        esum_ready = sem("esum_ready")
        erec_ready = sem("erec_ready")
        prefix_done = sem("prefix_done")
        place_a = sem("place_a")
        place_ready = sem("place_ready")
        gates_ready = sem("gates_ready")
        most_ready = sem("most_ready")
        flag_ready = sem("flag_ready")
        gu_in = [sem(f"gu_in{j}") for j in range(16)]
        dn_in = [sem(f"dn_in{j}") for j in range(4)]
        bias_in = [sem(f"bias_in{i}") for i in range(2)]
        gu_used = sem("gu_used")
        dn_used = sem("dn_used")
        pick_made = sem("pick_made")
        weigh_made = sem("weigh_made")
        gathered = sem("gathered")
        turned = sem("turned")
        xg_ready = sem("xg_ready")
        spread_ready = sem("spread_ready")
        clamped = sem("clamped")
        sig_ready = sem("sig_ready")
        gated = sem("gated")
        act_ready = sem("act_ready")
        act_turned = sem("act_turned")
        actT_ready = sem("actT_ready")
        y_ready = sem("y_ready")
        scattered = sem("scattered")
        h_added = sem("h_added")
        place_moved = sem("place_moved")
        gfin_in = sem("gfin_in")
        out_ready = sem("out_ready")
        stored = sem("stored")

        AHEAD = (11, 9, 7, 5, 3, 1)
        NP = 28
        STEPS = PAIRS + 2 * E

        block = ctx.enter_context(nc.Block())

        @block.sync
        def _(sp):
            for t in range(TT):
                sp.dma_start(h[:, t, :], x[0, t * P:(t + 1) * P, :]).then_inc(x_in[t], 16)
            sp.dma_start(meta, meta_tokens).then_inc(meta_in, 16)
            sp.wait_ge(stage_clear, 1)
            for name in ON_SP:
                r0, k, ap = rows[name]
                sp.dma_start(stage[r0:r0 + k, 0, :], ap.rearrange("o (r c) -> (o r) c", c=P)).then_inc(stage_in, 16)
            sp.dma_start(stage[0:TAPS * CC, 1, :], w_dwconv.rearrange("o k (r c) -> (o k r) c", c=P)
                         ).then_inc(stage_in, 16)

            def load_block(i, j, part):
                c0 = BLOCKS[i][1]
                w = 512 // part
                for q in range(part):
                    sp.dma_start(win_block(i)[:, :, q * w:(q + 1) * w],
                                 w_in[0, :, c0 + q * w:c0 + (q + 1) * w].rearrange("(k p) n -> p k n", p=P)
                                 ).then_inc(win_in[j + q], 16)

            load_block(0, 0, 2)
            load_block(1, 2, 1)
            sp.dma_start(wpool, w_pool_grp[0].rearrange("g p n -> p g n")).then_inc(wpool_in, 16)
            for i in range(2, 7):
                load_block(i, i + 1, 1)
            sp.dma_start(rw[:, :, :], router_w[0].rearrange("(k p) e -> p k e", p=P)).then_inc(router_in, 16)
            sp.dma_start(rb[:, :], router_b[0].partition_broadcast(P)).then_inc(router_in, 16)
            sp.dma_start(pw2_sb, w_pw2[0].rearrange("(c p) n -> p c n", p=P)).then_inc(pw2_in, 16)
            sp.wait_ge(proj_done, 8)
            sp.dma_start(wout_sb, w_out[0].rearrange("(c p) n -> p c n", p=P)).then_inc(wout_in, 16)

            def load_gu(e, j):
                k = j % KC
                sp.dma_start(gu_ring[:, j, :], w_gate_up[0, e, k * P:(k + 1) * P, :]).then_inc(gu_in[j], 16)

            def load_dn(e, f):
                sp.dma_start(dn_ring[:, f, :].rearrange("p (j n) -> p j n", j=2),
                             w_down[0, e, 2 * f * P:2 * (f + 1) * P, :].rearrange("(j p) n -> p j n", p=P)
                             ).then_inc(dn_in[f], 16)

            def load_bias(e, i):
                sp.dma_start(bias[0:4, i, :], b_gate_up[0, e, :].rearrange("(r c) -> r c", c=512)
                             ).then_inc(bias_in[i], 16)
                sp.dma_start(bias[4:6, i, :], b_down[0, e, :].rearrange("(r c) -> r c", c=512)
                             ).then_inc(bias_in[i], 16)

            load_bias(0, 0)
            load_bias(1, 1)
            for j in range(16):
                if j < 10 and j % 2 == 0:
                    sp.wait_ge(proj_done, 12 + 4 * (j // 2))
                if j == 10:
                    sp.wait_ge(pw2_done, 4)
                if j == 12:
                    sp.wait_ge(wout_done, 4)
                load_gu(j // KC, j)
            sp.wait_ge(logits_done, TT)
            sp.wait_ge(place_ready, 1)
            sp.wait_ge(gates_ready, TT)
            for f in range(4):
                load_dn(0, f)

            def load_gu_of(e, i, n, k):
                sp.wait_ge(gu_used, 16 * (n - 1) + i * KC + k + 1)
                load_gu(e, i * KC + k)

            def load_bias_of(e, i, n):
                sp.wait_ge(dn_used, 8 * (n - 1) + 4 * i + 1)
                load_bias(e, i)

            def load_dn_of(e, i, n):
                for f in range(4):
                    sp.wait_ge(dn_used, 8 * n + 4 * (i - 1) + f + 1)
                    load_dn(e, f)

            def load_step(n, ahead=0):
                for j in range(2 * KC):
                    if j == ahead:
                        load_dn_of(2 * n - 1, 1, n - 1)
                    load_gu_of(2 * n + j // KC, j // KC, n, j % KC)
                    if j == max(KC - 1, ahead - 1):
                        load_bias_of(2 * n, 0, n)
                load_bias_of(2 * n + 1, 1, n)
                load_dn_of(2 * n, 0, n)

            for n, ahead in enumerate(AHEAD, 1):
                load_step(n, ahead)
            with sp.Fori(1 + len(AHEAD), PAIRS) as n:
                load_step(n)
            load_dn_of(E - 1, 1, PAIRS - 1)
            sp.wait_ge(flag_ready, 1)
            over = sp.value_load(flag[0:1, 0:1], min_val=0, max_val=1)
            with sp.If(over):
                with sp.Fori(0, 2) as r:
                    with sp.Fori(0, E) as e:
                        n = PAIRS + E * r + e
                        for i in range(2):
                            for k in range(KC):
                                load_gu_of(e, i, n, k)
                            load_bias_of(e, i, n)
                        load_dn_of(e, 0, n)
                        load_dn_of(e, 1, n)
                sp.wait_ge(act_ready, 2 * STEPS)
            sp.wait_ge(act_ready, 2 * PAIRS)
            sp.dma_start(gfin, norm_final_g.partition_broadcast(P)).then_inc(gfin_in, 16)
            for t in range(TT):
                sp.wait_ge(out_ready, t + 1)
                sp.dma_start(out[0, t * P:(t + 1) * P, :], outb[:, t, :]).then_inc(stored, 16)
            sp.wait_ge(stored, 16 * TT)

        @block.gpsimd
        def _(pool):
            nc.gpsimd.memset(ident[:], 0.0).then_inc(consts_a, 1)
            nc.gpsimd.memset(ones[:], 1.0).then_inc(consts_a, 1)
            nc.gpsimd.memset(seg[:, :, :], 0.0).then_inc(consts_a, 1)
            pool.wait_ge(consts_a, 1)
            nc.gpsimd.affine_select(out=ident[:], in_=ident[:], compare_op=ALU.not_equal, fill=1.0, base=0,
                                    pattern=[[-1, P]], channel_multiplier=1).then_inc(consts_made, 1)
            pool.wait_ge(consts_a, 3)
            nc.gpsimd.affine_select(out=seg[:, :, :], in_=seg[:, :, :], compare_op=ALU.not_equal, fill=1.0, base=0,
                                    pattern=[[-1, 6], [0, SLOTS]], channel_multiplier=1).then_inc(consts_made, 1)
            nc.gpsimd.affine_select(out=earlier[:], in_=ones[:], compare_op=ALU.is_gt, fill=0.0, base=0,
                                    pattern=[[1, P]], channel_multiplier=-1).then_inc(consts_made, 1)
            nc.gpsimd.iota(iota[:], pattern=[[1, 2 * SLOTS]], base=0, channel_multiplier=0,
                           allow_small_or_imprecise_dtypes=True).then_inc(consts_made, 1)

            pool.wait_ge(proj_read, 12)
            pool.wait_ge(glu_ready, 4)
            src, dst = uT, sumA
            for lv in range(4):
                w = 1 << lv
                if lv:
                    pool.wait_ge(pool_step, lv)
                so, do = (1 if lv == 2 else 0), (1 if lv in (1, 3) else 0)
                so = 1 if lv in (2,) else 0
                lo = 2 * w - 1
                nc.gpsimd.tensor_tensor(dst[:, lv - do:CC - do, lo:L], src[:, lv - so:CC - so, lo:L],
                                        src[:, lv - so:CC - so, lo - w:L - w], ALU.add).then_inc(pool_step, 1)
                src, dst = (sumA, sumB) if lv % 2 == 0 else (sumB, sumA)
            pool.wait_ge(pool_step, 4)
            for g, w in enumerate(POOL_WINDOWS):
                s = (sumA[:, g, META:L] if g % 2 == 0 else sumB[:, g - 1, META:L])
                nc.gpsimd.tensor_scalar(s, s, 1.0 / w, None, ALU.mult).then_inc(pool_step, 1)
            for g in range(CC):
                s = (sumA[:, g, META:L] if g % 2 == 0 else sumB[:, g - 1, META:L])
                pool.wait_ge(pool_step, 5 + g)
                nc.gpsimd.tensor_tensor(uT[:, g, META:L], s, uT[:, g, META:L], ALU.subtract).then_inc(pooled, 1)
            for m in range(KC):
                pool.wait_ge(proj_read, 12 + m + 1)
                pool.wait_ge(ya_ready, m + 1)
                nc.gpsimd.tensor_tensor(mix[:, m, :], mix[:, m, :], gasig[:, m % 4, :], ALU.mult
                                        ).then_inc(ya_gated, 1)

        @block.scalar
        def _(act):
            act.wait_ge(stage_clear, 1)
            for name in ON_ACT:
                r0, k, ap = rows[name]
                act.dma_start(stage[r0:r0 + k, 0, :], ap.rearrange("o (r c) -> (o r) c", c=P)).then_inc(stage_in, 16)

            def root(i, k, rows_=P):
                act.wait_ge(meaned, k)
                nc.scalar.activation(ss[0:rows_, i:i + 1], ss[0:rows_, i:i + 1], ACT.Sqrt).then_inc(rooted, 1)

            for i in range(TT + 1):
                root(i, i + 1, P if i < TT else META)

            def evacuate(n, dst, func, name, m, w=SEQ):
                act.wait_ge(proj_done, n + 1)
                nc.scalar.activation(dst, ps[:, n % 4, 0:w], func, bias=col("b_in", m)).then_inc(proj_read, 1)

            act.wait_ge(par_ready, 1)
            for c in range(CC):
                evacuate(c, glu[:, c, PAD:LP], ACT.Identity, "b_in", CC + c, L)
            for c in range(CC):
                if c == 3:
                    act.wait_ge(glu_ready, 1)
                evacuate(4 + c, gtsig[:, c % 3, :], ACT.Sigmoid, "b_in", 2 * CC + c, L)
            for c in range(CC):
                evacuate(8 + c, uT[:, c, :], ACT.Identity, "b_in", c, L)
            for m in range(4):
                evacuate(12 + m, gasig[:, m, :], ACT.Sigmoid, "b_in", 3 * CC + m)
            for m in range(KC):
                act.wait_ge(pool_done, 2 * (m // 2) + 2)
                nc.scalar.activation(mix[:, m, :], ps[:, 4 + m // 2, (m % 2) * SEQ:(m % 2 + 1) * SEQ], ACT.Copy,
                                     scale=col("scale", m)).then_inc(ya_ready, 1)
            for m in range(4, KC):
                act.wait_ge(ya_gated, m - 3)
                evacuate(12 + m, gasig[:, m % 4, :], ACT.Sigmoid, "b_in", 3 * CC + m)
            for m in range(KC):
                evacuate(20 + m, gbsig[:, m, :], ACT.Sigmoid, "b_in", 3 * CC + KC + m)
                if m == 0:
                    act.wait_ge(centred, 1)
                    act.wait_ge(pooled, 4)
                    nc.scalar.activation(sq, conv, ACT.Square).then_inc(ln_squared, 1)
                if m == 2:
                    act.wait_ge(var_ready, 1)
                    nc.scalar.activation(lnr, lnr, ACT.Sqrt).then_inc(dev_ready, 1)
                if m == 4:
                    act.wait_ge(normed, 1)
                    for c in range(CC):
                        nc.scalar.activation(conv[:, c, :], conv[:, c, :], ACT.Identity, bias=col("ln_b", c),
                                             scale=col("ln_g", c)).then_inc(affine_done, 1)
                    act.wait_ge(affine_done, CC)
                    nc.scalar.activation(cvsig, conv, ACT.Sigmoid).then_inc(cvsig_ready, 1)

            for t in range(TT):
                root(3 + t, TT + 1 + t + 1)
            for t in range(TT):
                act.wait_ge(negmax_ready, t + 1)
                nc.scalar.activation(expl[:, t, :], logits[:, t, :], ACT.Exp, bias=negmax[:, t:t + 1]
                                     ).then_inc(exp_ready, 1)

            def step(n):
                act.wait_ge(turned, n + 1)
                nc.scalar.activation(spread[:, :, :], bank(6, 2, SEQ), ACT.Copy).then_inc(spread_ready, 1)
                for i in range(2):
                    act.wait_ge(clamped, 4 * n + 2 * i + 1)
                    nc.scalar.activation(sig[:, :], work[:, 0, :], ACT.Sigmoid, scale=SWIGLU_ALPHA
                                         ).then_inc(sig_ready, 1)
                    act.wait_ge(act_turned, 2 * n + i + 1)
                    nc.scalar.activation(actT[:, i, :, :], bank(4 + i, FC // 2, P), ACT.Copy).then_inc(actT_ready, 1)
                for i in range(2):
                    act.wait_ge(dn_used, 8 * n + 4 * (i + 1))
                    nc.scalar.activation(acts[:, i, :], ps[:, 6 + i, :], ACT.Copy).then_inc(y_ready, 1)

            with act.Fori(0, PAIRS) as n:
                step(n)
            act.wait_ge(h_added, 4 * PAIRS + 4)
            act.wait_ge(flag_ready, 1)
            over = act.value_load(flag[0:1, 0:1], min_val=0, max_val=1)
            with act.If(over):
                with act.Fori(PAIRS, STEPS) as n:
                    step(n)
                act.wait_ge(h_added, 4 * STEPS + 4)

            for t in range(TT):
                root(5 + t, 2 * TT + 1 + t + 1)

        @block.vector
        def _(dve):
            nc.vector.memset(stage, 0.0).then_inc(stage_clear, 1)
            nc.vector.memset(glu[:, :, 0:PAD], 0.0).then_inc(pads_made, 1)

            def mean(i, k, src, scratch, rows_=P):
                if k > 1:
                    dve.wait_ge(squared, k - 1)
                nc.vector.scalar_tensor_tensor(scratch, src, 1.0, src, ALU.mult, ALU.mult,
                                               accum_out=ss[0:rows_, i:i + 1]).then_inc(squared, 1)
                dve.wait_ge(squared, k)
                nc.vector.tensor_scalar(ss[0:rows_, i:i + 1], ss[0:rows_, i:i + 1], 1.0 / D, RMS_EPS, ALU.mult,
                                        ALU.add).then_inc(meaned, 1)

            def invert(i, k, rows_=P):
                dve.wait_ge(rooted, k)
                nc.vector.reciprocal(rstd[0:rows_, i:i + 1], ss[0:rows_, i:i + 1]).then_inc(inverted, 1)
                dve.wait_ge(inverted, k)

            for i in range(TT + 1):
                if i < TT:
                    dve.wait_ge(x_in[i], 16)
                    mean(i, i + 1, h[:, i, :], junk)
                else:
                    dve.wait_ge(meta_in, 16)
                    mean(i, i + 1, meta, junk[0:META, :], META)
            dve.wait_ge(par_turned, 1)
            nc.vector.tensor_copy(par[:, :, :], bank(2, 2, P)).then_inc(par_ready, 1)
            dve.wait_ge(par_ready, 1)
            for i in range(TT + 1):
                if i < TT:
                    invert(i, i + 1)
                    nc.vector.tensor_scalar(hs[:, i, :], h[:, i, :], rstd[:, i:i + 1], None, ALU.mult
                                            ).then_inc(scaled, 1)
                else:
                    invert(i, i + 1, META)
                    nc.vector.tensor_scalar(meta, meta, rstd[0:META, i:i + 1], None, ALU.mult).then_inc(scaled, 1)
            for q in range(2 * TT):
                t, hf = q // 2, q % 2
                dve.wait_ge(x_turned, q + 1)
                nc.vector.tensor_tensor(xnT[:, 4 * hf:4 * hf + 4, META + t * P:META + (t + 1) * P], bank(4 + q, 4, P),
                                        wide(col("g_mix", 4 * hf, 4), 4, P), ALU.mult).then_inc(xnT_ready, 1)
            dve.wait_ge(x_turned, 2 * TT + 1)
            nc.vector.tensor_tensor(xnT[:, :, 0:META], bank(0, KC, META), wide(col("g_mix", 0, KC), KC, META),
                                    ALU.mult).then_inc(xnT_ready, 1)

            for c in range(CC):
                dve.wait_ge(proj_read, 4 + c + 1)
                nc.vector.tensor_tensor(glu[:, c, PAD:LP], glu[:, c, PAD:LP], gtsig[:, c % 3, :], ALU.mult
                                        ).then_inc(glu_ready, 1)
            dve.wait_ge(pads_made, 1)
            dve.wait_ge(glu_ready, 4)
            for k in range(TAPS):
                for c in range(CC):
                    if k == 0:
                        ins = nc.vector.tensor_scalar(conv[:, c, :], glu[:, c, 0:SEQ], tap(0, c), col("b_dw", c),
                                                      ALU.mult, ALU.add)
                    else:
                        dve.wait_ge(conv_step, CC * (k - 1) + c + 1)
                        ins = nc.vector.scalar_tensor_tensor(conv[:, c, :], glu[:, c, k:k + SEQ], tap(k, c),
                                                             conv[:, c, :], ALU.mult, ALU.add)
                    ins.then_inc(conv_step, 1)
            dve.wait_ge(ln_summed, 1)
            nc.vector.scalar_tensor_tensor(conv, ps[:, 4, 0:SEQ].unsqueeze(1).to_broadcast([P, CC, SEQ]), -1.0 / CW,
                                           conv, ALU.mult, ALU.add).then_inc(centred, 1)
            dve.wait_ge(var_summed, 1)
            nc.vector.tensor_scalar(lnr, ps[:, 5, 0:SEQ], 1.0 / CW, LN_EPS, ALU.mult, ALU.add
                                    ).then_inc(var_ready, 1)
            dve.wait_ge(dev_ready, 1)
            nc.vector.reciprocal(lnr, lnr).then_inc(lnr_ready, 1)
            dve.wait_ge(lnr_ready, 1)
            nc.vector.tensor_tensor(conv, conv, lnr.unsqueeze(1).to_broadcast([P, CC, SEQ]), ALU.mult
                                    ).then_inc(normed, 1)
            dve.wait_ge(cvsig_ready, 1)
            nc.vector.tensor_tensor(conv, conv, cvsig, ALU.mult).then_inc(silu_ready, 1)
            dve.wait_ge(proj_read, NP)
            dve.wait_ge(ya_gated, KC)
            for q in range(KC // 2):
                dve.wait_ge(pw2_done, q + 1)
                for m in (2 * q, 2 * q + 1):
                    nc.vector.scalar_tensor_tensor(gbsig[:, m, :], ps[:, 4 + q, (m % 2) * SEQ:(m % 2 + 1) * SEQ],
                                                   col("b_pw2", m), gbsig[:, m, :], ALU.add, ALU.mult
                                                   ).then_inc(yb_gated, 1)
                dve.wait_ge(yb_gated, 2 * q + 2)
                nc.vector.tensor_tensor(mix[:, 2 * q:2 * q + 2, :], mix[:, 2 * q:2 * q + 2, :],
                                        gbsig[:, 2 * q:2 * q + 2, :], ALU.add).then_inc(mix_ready, 1)
            def turn_gain(t):
                for hf in range(2):
                    dve.wait_ge(hs_turned, 2 * t + hf + 1)
                    nc.vector.tensor_tensor(hT[:, 4 * hf:4 * hf + 4, t * P:(t + 1) * P], bank(4 + 2 * t + hf, 4, P),
                                            wide(col("g_ffn", 4 * hf, 4), 4, P), ALU.mult).then_inc(hT_ready, 1)

            for t in range(TT):
                for hf in range(2):
                    dve.wait_ge(wout_done, 2 * t + hf + 1)
                    nc.vector.tensor_tensor(h[:, t, hf * 512:(hf + 1) * 512], h[:, t, hf * 512:(hf + 1) * 512],
                                            ps[:, 2 * t + hf, :], ALU.add).then_inc(h_added, 1)
                if t == 0:
                    dve.wait_ge(h_added, 2)
                    mean(3, TT + 2, h[:, 0, :], junk_ffn)
                    invert(3, TT + 2)
                    nc.vector.tensor_scalar(hs[:, 0, :], h[:, 0, :], rstd[:, 3:4], None, ALU.mult).then_inc(scaled, 1)
                    turn_gain(0)
            turn_gain(1)
            dve.wait_ge(h_added, 4)
            mean(4, TT + 3, h[:, 1, :], junk_ffn)
            invert(4, TT + 3)
            nc.vector.tensor_scalar(hs[:, 1, :], h[:, 1, :], rstd[:, 4:5], None, ALU.mult).then_inc(scaled, 1)
            dve.wait_ge(scaled, 2 * TT + 1)
            dve.wait_ge(router_in, 32)
            dve.wait_ge(consts_made, 4)
            for t in range(TT):
                dve.wait_ge(logits_done, t + 1)
                nc.vector.scalar_tensor_tensor(logits[:, t, :], ps[:, t, 0:E], rstd[:, 3 + t:4 + t], rb, ALU.mult,
                                               ALU.add).then_inc(logits_ready, 1)
            for t in range(TT):
                dve.wait_ge(logits_ready, t + 1)
                nc.vector.max(top[:, t, :], logits[:, t, :]).then_inc(top_ready, 1)
            for t in range(TT):
                dve.wait_ge(top_ready, t + 1)
                nc.vector.max_index(topi[:, t, :], top[:, t, :], logits[:, t, :]).then_inc(topi_ready, 1)
                nc.vector.tensor_scalar(negmax[:, t:t + 1], top[:, t, 0:1], -1.0, None, ALU.mult
                                        ).then_inc(negmax_ready, 1)
            for t in range(TT):
                dve.wait_ge(topi_ready, t + 1)
                nc.vector.tensor_copy(topf[:, t, :], topi[:, t, :]).then_inc(topf_ready, 1)
            for k in range(TOP_K):
                for t in range(TT):
                    if k == 0:
                        dve.wait_ge(topf_ready, t + 1)
                        ins = nc.vector.tensor_scalar(chosen[:, t, 0, :], iota[:, 0:E], topf[:, t, 0:1], None,
                                                      ALU.is_equal)
                    else:
                        dve.wait_ge(chosen_step, TT * (k - 1) + t + 1)
                        ins = nc.vector.scalar_tensor_tensor(chosen[:, t, k, :], iota[:, 0:E], topf[:, t, k:k + 1],
                                                             chosen[:, t, k - 1, :], ALU.is_equal, ALU.add)
                    ins.then_inc(chosen_step, 1)
            dve.wait_ge(chosen_step, TT * TOP_K)
            for t in range(TT):
                dve.wait_ge(exp_ready, t + 1)
                nc.vector.scalar_tensor_tensor(expl[:, t, :], expl[:, t, :], 1.0, chosen[:, t, TOP_K - 1, :],
                                               ALU.mult, ALU.mult, accum_out=esum[:, t:t + 1]).then_inc(esum_ready, 1)
            dve.wait_ge(esum_ready, TT)
            nc.vector.reciprocal(erec[:, :], esum[:, :]).then_inc(erec_ready, 1)
            dve.wait_ge(erec_ready, 1)
            for t in range(TT):
                nc.vector.tensor_scalar(gates[:, t, 0:E], expl[:, t, :], erec[:, t:t + 1], None, ALU.mult
                                        ).then_inc(gates_ready, 1)
            dve.wait_ge(prefix_done, 1)
            for t in range(TT):
                nc.vector.scalar_tensor_tensor(place[:, t, 0:E], ps[:, 2, t * E:(t + 1) * E], 1.0,
                                               chosen[:, t, TOP_K - 1, :], ALU.add, ALU.mult).then_inc(place_a, 1)
            nc.vector.reduce_max(most[:, :], ps[0:1, 2, TT * E:(TT + 1) * E], AX_X).then_inc(most_ready, 1)
            dve.wait_ge(place_a, TT)
            nc.vector.tensor_scalar(place[:, :, 0:E], place[:, :, 0:E], -1.0, None, ALU.add).then_inc(place_ready, 1)
            dve.wait_ge(most_ready, 1)
            nc.vector.tensor_scalar(flag[:, :], most[:, :], float(SLOTS), None, ALU.is_gt).then_inc(flag_ready, 1)
            dve.wait_ge(gates_ready, TT)
            dve.wait_ge(place_ready, 1)

            iota_pair = iota[:, 0:SLOTS].unsqueeze(1).unsqueeze(1).to_broadcast([P, TT, 2, SLOTS])
            iota_one = iota[:, :].unsqueeze(1).to_broadcast([P, TT, 2 * SLOTS])

            def select_pair(n, e, first=False):
                if not first:
                    dve.wait_ge(gathered, 2 * n)
                nc.vector.tensor_tensor(pick[:, :, :].rearrange("p t (i s) -> p t i s", i=2), iota_pair,
                                        place[:, :, bass.ds(e, 2)].unsqueeze(3).to_broadcast([P, TT, 2, SLOTS]),
                                        ALU.is_equal).then_inc(pick_made, 1)
                if not first:
                    dve.wait_ge(turned, n)
                dve.wait_ge(pick_made, n + 1)
                for t in range(TT):
                    nc.vector.tensor_tensor(
                        weigh[:, t, :, :, :],
                        pick[:, t, :].rearrange("p (i s) -> p i s", i=2).unsqueeze(2).to_broadcast([P, 2, 2, SLOTS]),
                        gates[:, t, bass.ds(e, 2)].unsqueeze(2).unsqueeze(3).to_broadcast([P, 2, 2, SLOTS]),
                        ALU.mult).then_inc(weigh_made, 1)

            def select_one(n, e):
                dve.wait_ge(gathered, 2 * n)
                nc.vector.tensor_tensor(pick[:, :, :], iota_one,
                                        place[:, :, bass.ds(e, 1)].to_broadcast([P, TT, 2 * SLOTS]),
                                        ALU.is_equal).then_inc(pick_made, 1)
                dve.wait_ge(turned, n)
                dve.wait_ge(pick_made, n + 1)
                for t in range(TT):
                    nc.vector.tensor_tensor(
                        weigh[:, t, :, :, :],
                        pick[:, t, :].rearrange("p (i s) -> p i s", i=2).unsqueeze(2).to_broadcast([P, 2, 2, SLOTS]),
                        gates[:, t, bass.ds(e, 1)].unsqueeze(2).unsqueeze(3).to_broadcast([P, 2, 2, SLOTS]),
                        ALU.mult).then_inc(weigh_made, 1)

            def gather_gain(n):
                for q in range(2):
                    dve.wait_ge(gathered, 2 * n + q + 1)
                    nc.vector.tensor_tensor(xg[:, 4 * q:4 * q + 4, :], bank(4 + q, 4, P),
                                            wide(col("g_ffn", 4 * q, 4), 4, P), ALU.mult).then_inc(xg_ready, 1)

            def swiglu(n, i):
                dve.wait_ge(gu_used, 16 * n + 8 * (i + 1))
                if i:
                    dve.wait_ge(act_ready, 2 * n + i)
                nc.vector.tensor_scalar(work[:, 0, :], ps[:, 2 * i, :], SWIGLU_LIMIT, None, ALU.min
                                        ).then_inc(clamped, 1)
                nc.vector.tensor_scalar(work[:, 1, :], ps[:, 2 * i + 1, :], SWIGLU_LIMIT, -SWIGLU_LIMIT, ALU.min,
                                        ALU.max).then_inc(clamped, 1)
                dve.wait_ge(sig_ready, 2 * n + i + 1)
                nc.vector.tensor_tensor(sig[:, :], work[:, 0, :], sig[:, :], ALU.mult).then_inc(gated, 1)
                dve.wait_ge(gated, 2 * n + i + 1)
                dve.wait_ge(clamped, 4 * n + 2 * i + 2)
                nc.vector.scalar_tensor_tensor(acts[:, i, :], work[:, 1, :], 1.0, sig[:, :], ALU.add, ALU.mult
                                               ).then_inc(act_ready, 1)

            def add_outputs(n):
                for q in range(4):
                    t, hf = q // 2, q % 2
                    dve.wait_ge(scattered, 4 * n + q + 1)
                    if q == 0:
                        dve.wait_ge(h_added, 4 * n + 4)
                    nc.vector.tensor_tensor(h[:, t, hf * 512:(hf + 1) * 512], h[:, t, hf * 512:(hf + 1) * 512],
                                            ps[:, q, :], ALU.add).then_inc(h_added, 1)

            select_pair(0, 0, first=True)
            with dve.Fori(0, PAIRS - 1) as n:
                gather_gain(n)
                swiglu(n, 0)
                select_pair(n + 1, 2 * n + 2)
                swiglu(n, 1)
                add_outputs(n)
            gather_gain(PAIRS - 1)
            swiglu(PAIRS - 1, 0)
            swiglu(PAIRS - 1, 1)
            add_outputs(PAIRS - 1)
            dve.wait_ge(h_added, 4 * PAIRS + 4)
            dve.wait_ge(flag_ready, 1)
            over = dve.value_load(flag[0:1, 0:1], min_val=0, max_val=1)
            with dve.If(over):
                for r in range(2):
                    nc.vector.tensor_scalar(place[:, :, :], place[:, :, :], -float(SLOTS * (r + 1)), None, ALU.add
                                            ).then_inc(place_moved, 1)
                    dve.wait_ge(place_moved, r + 1)
                    with dve.Fori(0, E) as e:
                        n = PAIRS + r * E + e
                        select_one(n, e)
                        gather_gain(n)
                        swiglu(n, 0)
                        swiglu(n, 1)
                        add_outputs(n)
                dve.wait_ge(h_added, 4 * STEPS + 4)

            for t in range(TT):
                mean(5 + t, 2 * TT + 1 + t + 1, h[:, t, :], junk2)
                invert(5 + t, 2 * TT + 1 + t + 1)
                if t == 0:
                    dve.wait_ge(gfin_in, 16)
                nc.vector.scalar_tensor_tensor(outb[:, t, :], h[:, t, :], rstd[:, 5 + t:6 + t], gfin,
                                               ALU.mult, ALU.mult).then_inc(out_ready, 1)

        @block.tensor
        def _(pe):
            mm = nc.tensor.matmul
            pe.wait_ge(consts_made, 1)
            pe.wait_ge(stage_in, 16 * (len(rows) + 1))
            for i in range(2):
                ins = nc.tensor.transpose(ps[:, 2, i * P:(i + 1) * P], stage[:, i, :], ident[:])
            ins.then_inc(par_turned, 1)
            for q in range(2 * TT):
                pe.wait_ge(scaled, q // 2 + 1)
                for i in range(4):
                    c = 4 * (q % 2) + i
                    ins = nc.tensor.transpose(ps[:, 4 + q, i * P:(i + 1) * P], hs[:, q // 2, c * P:(c + 1) * P],
                                              ident[:])
                ins.then_inc(x_turned, 1)
            pe.wait_ge(scaled, TT + 1)
            for c in range(KC):
                ins = nc.tensor.transpose(ps[:, 0, c * META:(c + 1) * META], meta[:, c * P:(c + 1) * P],
                                          ident[0:META, 0:META])
            ins.then_inc(x_turned, 1)

            pe.wait_ge(xnT_ready, 2 * TT + 1)

            def project(n):
                i, q = n // 4, n % 4
                if n in (0, 2):
                    pe.wait_ge(win_in[n // 2], 16)
                elif n % 4 == 0:
                    pe.wait_ge(win_in[i + 1], 16)
                if n >= 4:
                    pe.wait_ge(proj_read, n - 3)
                lo = 0 if n < 12 else META
                for k in range(KC):
                    ins = mm(ps[:, q, 0:L - lo], win_block(i)[:, k, q * P:(q + 1) * P], xnT[:, k, lo:L],
                             start=k == 0, stop=k == KC - 1)
                ins.then_inc(proj_done, 1)

            for n in range(16):
                project(n)
            pe.wait_ge(wpool_in, 16)
            for m in range(KC):
                g = m // 2
                pe.wait_ge(pooled, g + 1)
                mm(ps[:, 4 + m // 2, (m % 2) * SEQ:(m % 2 + 1) * SEQ], wpool[:, g, (m % 2) * P:(m % 2 + 1) * P],
                   uT[:, g, META:L], start=True, stop=True).then_inc(pool_done, 1)
            for n in range(16, 21):
                project(n)
            pe.wait_ge(consts_made, 4)
            pe.wait_ge(ya_ready, KC)
            for c in range(CC):
                pe.wait_ge(conv_step, CC * (TAPS - 1) + c + 1)
                ins = mm(ps[:, 4, 0:SEQ], ones[:], conv[:, c, :], start=c == 0, stop=c == CC - 1)
            ins.then_inc(ln_summed, 1)
            for n in range(21, 22):
                project(n)
            pe.wait_ge(ln_squared, 1)
            for c in range(CC):
                ins = mm(ps[:, 5, 0:SEQ], ones[:], sq[:, c, :], start=c == 0, stop=c == CC - 1)
            ins.then_inc(var_summed, 1)
            for n in range(22, NP):
                project(n)
            pe.wait_ge(pw2_in, 16)
            pe.wait_ge(silu_ready, 1)
            for m in range(KC):
                for c in range(CC):
                    ins = mm(ps[:, 4 + m // 2, (m % 2) * SEQ:(m % 2 + 1) * SEQ], pw2_sb[:, c, m * P:(m + 1) * P],
                             conv[:, c, :], start=c == 0, stop=c == CC - 1)
                if m % 2:
                    ins.then_inc(pw2_done, 1)
            pe.wait_ge(wout_in, 16)
            pe.wait_ge(proj_read, NP)
            for t in range(TT):
                for m in range(KC):
                    if t == 0:
                        pe.wait_ge(mix_ready, m // 2 + 1)
                    for hf in range(2):
                        ins = mm(ps[:, 2 * t + hf, :], mix[:, m, t * P:(t + 1) * P],
                                 wout_sb[:, m, hf * 512:(hf + 1) * 512], start=m == 0, stop=m == KC - 1)
                        if m == KC - 1:
                            ins.then_inc(wout_done, 1)
            for q in range(2 * TT):
                pe.wait_ge(h_added, q + 1)
                for i in range(4):
                    c = 4 * (q % 2) + i
                    ins = nc.tensor.transpose(ps[:, 4 + q, i * P:(i + 1) * P], h[:, q // 2, c * P:(c + 1) * P],
                                              ident[:])
                ins.then_inc(hs_turned, 1)
            pe.wait_ge(router_in, 32)
            for t in range(TT):
                pe.wait_ge(hT_ready, 2 * t + 2)
                for k in range(KC):
                    ins = mm(ps[:, t, 0:E], hT[:, k, t * P:(t + 1) * P], rw[:, k, :], start=k == 0, stop=k == KC - 1)
                ins.then_inc(logits_done, 1)
            pe.wait_ge(chosen_step, TT * TOP_K)
            last = [chosen[:, t, TOP_K - 1, :] for t in range(TT)]
            mm(ps[:, 2, 0:E], earlier[:], last[0], start=True, stop=True)
            mm(ps[:, 2, E:2 * E], earlier[:], last[1], start=True, stop=False)
            mm(ps[:, 2, E:2 * E], ones[:], last[0], start=False, stop=True)
            mm(ps[:, 2, 2 * E:3 * E], ones[:], last[0], start=True, stop=False)
            mm(ps[:, 2, 2 * E:3 * E], ones[:], last[1], start=False, stop=True).then_inc(prefix_done, 1)

            def step(n):
                pe.wait_ge(pick_made, n + 1)
                for c in range(KC):
                    for t in range(TT):
                        ins = mm(ps[:, 4 + c // 4, (c % 4) * P:(c % 4 + 1) * P], hs[:, t, c * P:(c + 1) * P],
                                 pick[:, t, :], start=t == 0, stop=t == TT - 1)
                    if c % 4 == 3:
                        ins.then_inc(gathered, 1)
                def turn_weights():
                    pe.wait_ge(weigh_made, 2 * n + 2)
                    for i in range(2):
                        for t in range(TT):
                            ins = nc.tensor.transpose(ps[:, 6, i * SEQ + t * P:i * SEQ + (t + 1) * P],
                                                      weigh[:, t, i, :, :].rearrange("p a b -> p (a b)"), ident[:])
                    ins.then_inc(turned, 1)

                def turn_acts(i):
                    pe.wait_ge(act_ready, 2 * n + i + 1)
                    for b in range(FC // 2):
                        ins = nc.tensor.transpose(ps[:, 4 + i, b * P:(b + 1) * P], acts[:, i, b * P:(b + 1) * P],
                                                  ident[:])
                    ins.then_inc(act_turned, 1)

                def scatter(i):
                    pe.wait_ge(y_ready, 2 * n + i + 1)
                    for t in range(TT):
                        for hf in range(2):
                            ins = mm(ps[:, 2 * t + hf, :], spread[hf * SLOTS:(hf + 1) * SLOTS, i, t * P:(t + 1) * P],
                                     acts[hf * SLOTS:(hf + 1) * SLOTS, i, :], start=i == 0, stop=i == 1)
                            if i == 1:
                                ins.then_inc(scattered, 1)

                pe.wait_ge(h_added, 4 * n + 4)
                for i in range(2):
                    for k in range(KC):
                        if i == 0 and k % 4 == 0:
                            pe.wait_ge(xg_ready, 2 * n + k // 4 + 1)
                        if k == KC - 1:
                            pe.wait_ge(bias_in[i], 32 * n + 32)
                            for g in range(2):
                                for hf in range(2):
                                    mm(ps[hf * SLOTS:(hf + 1) * SLOTS, 2 * i + g, :], seg[:, 2 * g + hf, :],
                                       bias[:, i, :], start=False, stop=False)
                        pe.wait_ge(gu_in[i * KC + k], 16 * n + 16)
                        for g in range(2):
                            for hf in range(2):
                                ins = mm(ps[hf * SLOTS:(hf + 1) * SLOTS, 2 * i + g, :],
                                         xg[:, k, i * SLOTS:(i + 1) * SLOTS],
                                         gu_ring[:, i * KC + k, g * F + hf * 512:g * F + (hf + 1) * 512],
                                         start=k == 0, stop=k == KC - 1)
                        ins.then_inc(gu_used, 1)
                        if i == 0 and k == 3:
                            turn_weights()
                        if i == 1 and k == 3:
                            turn_acts(0)
                pe.wait_ge(spread_ready, n + 1)
                for i in range(2):
                    pe.wait_ge(actT_ready, 2 * n + i + 1)
                    for hf in range(2):
                        mm(ps[hf * SLOTS:(hf + 1) * SLOTS, 6 + i, :], seg[:, 4 + hf, :], bias[:, i, :],
                           start=True, stop=False)
                    for f in range(4):
                        pe.wait_ge(dn_in[f], 32 * n + 16 * (i + 1))
                        for j in range(2):
                            c = 2 * f + j
                            for hf in range(2):
                                ins = mm(ps[hf * SLOTS:(hf + 1) * SLOTS, 6 + i, :],
                                         actT[:, i, c % 4, (c // 4) * SLOTS:(c // 4 + 1) * SLOTS],
                                         dn_ring[:, f, j * D + hf * 512:j * D + (hf + 1) * 512],
                                         start=False, stop=c == FC - 1)
                        ins.then_inc(dn_used, 1)
                        if i == 0 and f == 2:
                            turn_acts(1)
                        if i == 1 and f == 2:
                            scatter(0)
                scatter(1)

            with pe.Fori(0, PAIRS) as n:
                step(n)
            pe.wait_ge(flag_ready, 1)
            over = pe.value_load(flag[0:1, 0:1], min_val=0, max_val=1)
            with pe.If(over):
                with pe.Fori(PAIRS, STEPS) as n:
                    step(n)


_INS = ["x", "meta_tokens", "norm_mix_g", "w_in", "b_in", "w_pool_grp", "pool_scale", "w_dwconv", "b_dwconv",
        "conv_ln_g", "conv_ln_b", "w_pw2", "b_pw2", "w_out", "norm_ffn_g", "router_w", "router_b", "w_gate_up",
        "b_gate_up", "w_down", "b_down", "norm_final_g"]


def kernel(**inputs):
    import numpy as _np
    import concourse.bacc as _bacc
    from concourse import mybir as _mybir
    from concourse.bass_utils import run_bass_kernel_spmd as _run

    nc = _bacc.Bacc("TRN2", target_bir_lowering=False, num_devices=1)
    arrays, args = {}, []
    for name in _INS:
        a = _np.ascontiguousarray(inputs[name])
        arrays[f"in_{name}"] = a
        args.append(nc.dram_tensor(f"in_{name}", a.shape, _mybir.dt.from_np(a.dtype), kind="ExternalInput").ap())
    args.append(nc.dram_tensor("out_0", inputs["x"].shape, _mybir.dt.float32, kind="ExternalOutput").ap())
    block_kernel(nc, *args)
    r = _run(nc, [arrays], core_ids=[0])
    return r.results[0]["out_0"]
```

```python
from contextlib import ExitStack

import concourse.bass as bass
from concourse import mybir

ALU = mybir.AluOpType
ACT = mybir.ActivationFunctionType
F32 = mybir.dt.float32
I32 = mybir.dt.int32
U32 = mybir.dt.uint32
AX_X = mybir.AxisListType.X

P = 128
RMS_EPS = 1e-5
LN_EPS = 1e-5
SWIGLU_LIMIT = 7.0
SWIGLU_ALPHA = 1.702
TOP_K = 4
POOL_WINDOWS = (2, 4, 8, 16)
SLOTS = 64


def block_kernel(nc, x, meta_tokens, norm_mix_g, w_in, b_in, w_pool_grp, pool_scale, w_dwconv, b_dwconv,
                 conv_ln_g, conv_ln_b, w_pw2, b_pw2, w_out, norm_ffn_g, router_w, router_b, w_gate_up,
                 b_gate_up, w_down, b_down, norm_final_g, out):
    SEQ, D = x.shape[1], x.shape[2]
    META = meta_tokens.shape[0]
    L = SEQ + META
    CW = w_dwconv.shape[2]
    TAPS = w_dwconv.shape[1]
    E = router_w.shape[2]
    F = w_down.shape[2]
    KC = D // P
    FC = F // P
    CC = CW // P
    TT = SEQ // P
    PAIRS = E // 2
    PAD = TAPS - 1 - META
    LP = L + PAD
    assert (KC, FC, CC, TT, E) == (8, 8, 4, 2, 32) and PAD >= 0

    with ExitStack() as ctx:
        def sb(name, shape, dt=F32):
            return ctx.enter_context(nc.sbuf_tensor(name, shape, dt))

        def sem(name):
            return ctx.enter_context(nc.semaphore(name))

        gu_ring = sb("gu_ring", [P, 16, 2 * F])
        dn_ring = sb("dn_ring", [P, 4, 2 * D])
        h = sb("h", [P, TT, D])
        hs = sb("hs", [P, TT, D])
        mix = sb("mix", [P, 8, 256])
        work = sb("work", [P, 2, 512])
        sig = sb("sig", [P, 512])
        acts = sb("acts", [P, 2, 512])
        pick = sb("pick", [P, TT, 2 * SLOTS])
        weigh = sb("weigh", [P, TT, 2, 2, SLOTS])
        spread = sb("spread", [P, 2, SEQ])
        par = sb("par", [P, 2, P])
        bias = sb("bias", [6, 2, 512])
        seg = sb("seg", [6, 6, SLOTS])
        ident = sb("ident", [P, P])
        expert_no = sb("expert_no", [P, E])
        slot_no = sb("slot_no", [P, 2 * SLOTS])
        ss = sb("ss", [P, 8])
        rstd = sb("rstd", [P, 8])
        top = sb("top", [P, TT, 8])
        topi = sb("topi", [P, TT, 8], U32)
        topf = sb("topf", [P, TT, 8])
        negmax = sb("negmax", [P, TT])
        esum = sb("esum", [P, TT])
        erec = sb("erec", [P, TT])
        gates = sb("gates", [P, TT, E])
        place = sb("place", [P, TT, E])
        most = sb("most", [1, 1])
        spare = sb("spare", [P, 1])
        flag = sb("flag", [1, 1], I32)
        ps = ctx.enter_context(nc.psum_tensor("ps", [P, 8, 512], F32))

        weighf = weigh[:, :, :, :, :].rearrange("p a b c d -> p (a b c d)")
        ones = weighf[:, 0:P]
        earlier = weighf[:, P:2 * P]
        logits = weighf[:, 256:256 + TT * E].rearrange("p (t e) -> p t e", t=TT)
        expl = weighf[:, 320:320 + TT * E].rearrange("p (t e) -> p t e", t=TT)
        rb = weighf[:, 384:384 + E]

        xg = mix[:, 0:4, :].rearrange("p a b -> p (a b)").rearrange("p (c s) -> p c s", s=2 * SLOTS)
        actT = mix[:, 4:8, :].rearrange("p a b -> p (a b)").rearrange("p (i b s) -> p i b s", i=2, b=FC // 2)
        junk_ffn = work[:, :, :].rearrange("p a b -> p (a b)")
        dnf = dn_ring[:, :, :].rearrange("p a b -> p (a b)")
        cut = [0]

        def take(a, b):
            o = cut[0]
            cut[0] += a * b
            assert cut[0] <= 8 * D
            return dnf[:, o:o + a * b].rearrange("p (a b) -> p a b", b=b)

        xnT = take(KC, L)
        glu = take(CC, LP)
        uT = take(CC, L)
        wpool = take(CC, 256)
        conv = take(CC, SEQ)
        sumA = take(CC, L)
        sq = sumA[:, :, :].rearrange("p a b -> p (a b)")[:, 0:CC * SEQ].rearrange("p (a b) -> p a b", b=SEQ)
        cvsig = uT[:, :, :].rearrange("p a b -> p (a b)")[:, 0:CC * SEQ].rearrange("p (a b) -> p a b", b=SEQ)
        hT = xnT[:, :, 0:SEQ]
        rw = take(KC, E)
        chosen = take(TT * TOP_K, E).rearrange("p (t k) e -> p t k e", t=TT)
        lgT = sig[:, 0:SEQ]
        lnr = spread[:, 0, :]
        workf = work[:, :, :].rearrange("p a b -> p (a b)")
        gtsig = workf[:, 0:3 * L].rearrange("p (a b) -> p a b", b=L)
        sumB = workf[:, 0:3 * L].rearrange("p (a b) -> p a b", b=L)
        gasig = acts[:, :, :].rearrange("p a b -> p (a b)").rearrange("p (a b) -> p a b", b=SEQ)
        stage = acts[:, 0, 0:2 * P].rearrange("p (a b) -> p a b", b=P)
        gbsig = hs[:, :, :].rearrange("p a b -> p (a b)").rearrange("p (a b) -> p a b", b=SEQ)
        mixf = mix[:, :, :].rearrange("p a b -> p (a b)")
        meta = mixf[0:META, 0:D]
        junk = mixf[:, D:2 * D]

        rows = {}
        n = 0
        for name, ap in (("b_in", b_in), ("b_dw", b_dwconv), ("ln_g", conv_ln_g), ("ln_b", conv_ln_b),
                         ("b_pw2", b_pw2), ("scale", pool_scale), ("g_mix", norm_mix_g), ("g_ffn", norm_ffn_g)):
            k = ap.shape[1] // P
            rows[name] = (n, k, ap)
            n += k
        assert n <= P and TAPS * CC <= P
        ON_ACT = ("g_mix", "b_in", "b_dw", "ln_g")
        ON_SP = ("ln_b", "b_pw2", "scale", "g_ffn")

        def col(name, m, k=1):
            o = rows[name][0] + m
            return par[:, 0, o:o + k]

        def tap(k, c):
            return par[:, 1, k * CC + c:k * CC + c + 1]

        def wide(ap, k, w):
            return ap.unsqueeze(2).to_broadcast([P, k, w])

        def bank(b, a, w):
            return ps[:, b, 0:a * w].rearrange("p (a w) -> p a w", w=w)

        BLOCKS = [("v", CW, 12), ("gt", 2 * CW, 14), ("u", 0, 0), ("gA", 3 * CW, 2), ("gA", 3 * CW + 512, 4),
                  ("gB", 3 * CW + D, 6), ("gB", 3 * CW + D + 512, 8)]

        def win_block(i):
            s = BLOCKS[i][2]
            return gu_ring[:, s:s + 2, :].rearrange("p a b -> p (a b)").rearrange("p (k n) -> p k n", n=512)

        pw2_sb = gu_ring[:, 10:12, :].rearrange("p a b -> p (a b)").rearrange("p (c n) -> p c n", n=D)
        wout_sb = gu_ring[:, 12:16, :].rearrange("p a b -> p (a b)").rearrange("p (c n) -> p c n", n=D)
        gfin = workf
        outb = gu_ring[:, 1:3, 0:D]

        x_in = [sem(f"x_in{t}") for t in range(TT)]
        meta_in = sem("meta_in")
        stage_clear = sem("stage_clear")
        stage_in = sem("stage_in")
        wpool_in = sem("wpool_in")
        router_in = sem("router_in")
        win_in = [sem(f"win_in{i}") for i in range(8)]
        pw2_in = sem("pw2_in")
        wout_in = sem("wout_in")
        consts_a = sem("consts_a")
        consts_made = sem("consts_made")
        squared = sem("squared")
        squared_act = sem("squared_act")
        meaned = sem("meaned")
        rooted = sem("rooted")
        table_in = sem("table_in")
        inverted = sem("inverted")
        scaled = sem("scaled")
        x_turned = sem("x_turned")
        par_turned = sem("par_turned")
        par_ready = sem("par_ready")
        xnT_ready = sem("xnT_ready")
        xnT_act = sem("xnT_act")
        hs_ready = sem("hs_ready")
        pads_made = sem("pads_made")
        proj_done = sem("proj_done")
        proj_read = sem("proj_read")
        glu_ready = sem("glu_ready")
        conv_step = sem("conv_step")
        pool_step = sem("pool_step")
        pooled = sem("pooled")
        pool_done = sem("pool_done")
        ya_ready = sem("ya_ready")
        ya_gated = sem("ya_gated")
        ln_summed = sem("ln_summed")
        centred = sem("centred")
        ln_squared = sem("ln_squared")
        var_summed = sem("var_summed")
        var_ready = sem("var_ready")
        dev_ready = sem("dev_ready")
        lnr_ready = sem("lnr_ready")
        normed = sem("normed")
        affine_done = sem("affine_done")
        cvsig_ready = sem("cvsig_ready")
        silu_ready = sem("silu_ready")
        pw2_done = sem("pw2_done")
        yb_gated = sem("yb_gated")
        mix_ready = sem("mix_ready")
        wout_done = sem("wout_done")
        hs_turned = sem("hs_turned")
        hT_ready = sem("hT_ready")
        logits_done = sem("logits_done")
        groups_ready = sem("groups_ready")
        logits_turned = sem("logits_turned")
        logits_summed = sem("logits_summed")
        logits_ready = sem("logits_ready")
        top_ready = sem("top_ready")
        topi_ready = sem("topi_ready")
        topf_ready = sem("topf_ready")
        negmax_ready = sem("negmax_ready")
        exp_ready = sem("exp_ready")
        chosen_step = sem("chosen_step")
        esum_ready = sem("esum_ready")
        erec_ready = sem("erec_ready")
        prefix_done = sem("prefix_done")
        counts_done = sem("counts_done")
        place_ready = sem("place_ready")
        gates_ready = sem("gates_ready")
        most_ready = sem("most_ready")
        flag_ready = sem("flag_ready")
        gu_in = [sem(f"gu_in{j}") for j in range(16)]
        dn_in = [sem(f"dn_in{j}") for j in range(4)]
        bias_in = [sem(f"bias_in{i}") for i in range(2)]
        gu_used = sem("gu_used")
        dn_used = sem("dn_used")
        pick_made = sem("pick_made")
        weigh_made = sem("weigh_made")
        gathered = sem("gathered")
        turned = sem("turned")
        xg_ready = sem("xg_ready")
        spread_ready = sem("spread_ready")
        clamped = sem("clamped")
        sig_ready = sem("sig_ready")
        gated = sem("gated")
        act_ready = sem("act_ready")
        act_turned = sem("act_turned")
        actT_ready = sem("actT_ready")
        y_ready = sem("y_ready")
        scattered = sem("scattered")
        h_added = sem("h_added")
        place_moved = sem("place_moved")
        gfin_in = sem("gfin_in")
        out_ready = sem("out_ready")
        stored = sem("stored")

        AHEAD = range(11, 0, -2)
        NP = 28
        STEPS = PAIRS + 2 * E

        block = ctx.enter_context(nc.Block())

        @block.sync
        def _(sp):
            for t in range(TT):
                sp.dma_start(h[:, t, :], x[0, t * P:(t + 1) * P, :]).then_inc(x_in[t], 16)
            sp.dma_start(meta, meta_tokens).then_inc(meta_in, 16)
            sp.wait_ge(stage_clear, 1)
            sp.dma_start(stage[0:TAPS * CC, 1, :], w_dwconv.rearrange("o k (r c) -> (o k r) c", c=P)
                         ).then_inc(stage_in, 16)
            for name in ON_SP:
                r0, k, ap = rows[name]
                sp.dma_start(stage[r0:r0 + k, 0, :], ap.rearrange("o (r c) -> (o r) c", c=P)).then_inc(stage_in, 16)

            def load_block(i, j, part):
                c0 = BLOCKS[i][1]
                w = 512 // part
                for q in range(part):
                    sp.dma_start(win_block(i)[:, :, q * w:(q + 1) * w],
                                 w_in[0, :, c0 + q * w:c0 + (q + 1) * w].rearrange("(k p) n -> p k n", p=P)
                                 ).then_inc(win_in[j + q], 16)

            load_block(0, 0, 2)
            load_block(1, 2, 1)
            sp.dma_start(wpool, w_pool_grp[0].rearrange("g p n -> p g n")).then_inc(wpool_in, 16)
            for i in range(2, 7):
                load_block(i, i + 1, 1)
            sp.dma_start(rw[:, :, :], router_w[0].rearrange("(k p) e -> p k e", p=P)).then_inc(router_in, 16)
            sp.dma_start(rb[:, :], router_b[0].partition_broadcast(P)).then_inc(router_in, 16)
            sp.dma_start(pw2_sb, w_pw2[0].rearrange("(c p) n -> p c n", p=P)).then_inc(pw2_in, 16)
            sp.wait_ge(proj_done, 8)
            sp.dma_start(wout_sb, w_out[0].rearrange("(c p) n -> p c n", p=P)).then_inc(wout_in, 16)

            def load_gu(e, j):
                k = j % KC
                sp.dma_start(gu_ring[:, j, :], w_gate_up[0, e, k * P:(k + 1) * P, :]).then_inc(gu_in[j], 16)

            def load_dn(e, f):
                sp.dma_start(dn_ring[:, f, :].rearrange("p (j n) -> p j n", j=2),
                             w_down[0, e, 2 * f * P:2 * (f + 1) * P, :].rearrange("(j p) n -> p j n", p=P)
                             ).then_inc(dn_in[f], 16)

            def load_bias(e, i):
                sp.dma_start(bias[0:4, i, :], b_gate_up[0, e, :].rearrange("(r c) -> r c", c=512)
                             ).then_inc(bias_in[i], 16)
                sp.dma_start(bias[4:6, i, :], b_down[0, e, :].rearrange("(r c) -> r c", c=512)
                             ).then_inc(bias_in[i], 16)

            load_bias(0, 0)
            load_bias(1, 1)
            for j in range(16):
                if j < 10 and j % 2 == 0:
                    sp.wait_ge(proj_done, 12 + 4 * (j // 2))
                if j == 10:
                    sp.wait_ge(pw2_done, 4)
                if j == 12:
                    sp.wait_ge(wout_done, 4)
                load_gu(j // KC, j)
            sp.wait_ge(logits_done, 1)
            sp.wait_ge(place_ready, TT)
            sp.wait_ge(gates_ready, TT)
            sp.wait_ge(counts_done, 1)
            for f in range(4):
                load_dn(0, f)

            def load_gu_of(e, i, n, k):
                sp.wait_ge(gu_used, 16 * (n - 1) + i * KC + k + 1)
                load_gu(e, i * KC + k)

            def load_bias_of(e, i, n):
                sp.wait_ge(dn_used, 8 * (n - 1) + 4 * i + 1)
                load_bias(e, i)

            def load_dn_of(e, i, n):
                for f in range(4):
                    sp.wait_ge(dn_used, 8 * n + 4 * (i - 1) + f + 1)
                    load_dn(e, f)

            def load_step(n, ahead=0):
                for j in range(2 * KC):
                    if j == ahead:
                        load_dn_of(2 * n - 1, 1, n - 1)
                    load_gu_of(2 * n + j // KC, j // KC, n, j % KC)
                    if j == max(KC - 1, ahead - 1):
                        load_bias_of(2 * n, 0, n)
                load_bias_of(2 * n + 1, 1, n)
                load_dn_of(2 * n, 0, n)

            for n, ahead in enumerate(AHEAD, 1):
                load_step(n, ahead)
            with sp.Fori(1 + len(AHEAD), PAIRS) as n:
                load_step(n)
            load_dn_of(E - 1, 1, PAIRS - 1)
            sp.wait_ge(flag_ready, 1)
            over = sp.value_load(flag[0:1, 0:1], min_val=0, max_val=1)
            with sp.If(over):
                with sp.Fori(0, 2) as r:
                    with sp.Fori(0, E) as e:
                        n = PAIRS + E * r + e
                        for i in range(2):
                            for k in range(KC):
                                load_gu_of(e, i, n, k)
                            load_bias_of(e, i, n)
                        load_dn_of(e, 0, n)
                        load_dn_of(e, 1, n)
                sp.wait_ge(act_ready, 2 * STEPS)
            sp.wait_ge(act_ready, 2 * PAIRS)
            sp.dma_start(gfin, norm_final_g.partition_broadcast(P)).then_inc(gfin_in, 16)
            for t in range(TT):
                for hf in range(2):
                    cols = slice(hf * 512, (hf + 1) * 512)
                    sp.wait_ge(out_ready, 2 * t + hf + 1)
                    sp.dma_start(out[0, t * P:(t + 1) * P, cols], outb[:, t, cols]).then_inc(stored, 16)
            sp.wait_ge(stored, 16 * 2 * TT)

        @block.gpsimd
        def _(pool):
            nc.gpsimd.memset(ident[:], 0.0).then_inc(consts_a, 1)
            nc.gpsimd.memset(ones[:], 1.0).then_inc(consts_a, 1)
            nc.gpsimd.memset(seg[:, :, :], 0.0).then_inc(consts_a, 1)
            pool.wait_ge(consts_a, 1)
            nc.gpsimd.affine_select(out=ident[:], in_=ident[:], compare_op=ALU.not_equal, fill=1.0, base=0,
                                    pattern=[[-1, P]], channel_multiplier=1).then_inc(consts_made, 1)
            pool.wait_ge(consts_a, 3)
            nc.gpsimd.affine_select(out=seg[:, :, :], in_=seg[:, :, :], compare_op=ALU.not_equal, fill=1.0, base=0,
                                    pattern=[[-1, 6], [0, SLOTS]], channel_multiplier=1).then_inc(consts_made, 1)
            nc.gpsimd.affine_select(out=earlier[:], in_=ones[:], compare_op=ALU.is_gt, fill=0.0, base=0,
                                    pattern=[[1, P]], channel_multiplier=-1).then_inc(consts_made, 1)
            nc.gpsimd.iota(slot_no[:], pattern=[[1, 2 * SLOTS]], base=1, channel_multiplier=0,
                           allow_small_or_imprecise_dtypes=True).then_inc(consts_made, 1)
            nc.gpsimd.iota(expert_no[:], pattern=[[1, E]], base=0, channel_multiplier=0,
                           allow_small_or_imprecise_dtypes=True).then_inc(consts_made, 1)

            pool.wait_ge(proj_read, 12)
            pool.wait_ge(glu_ready, 4)
            src, dst = uT, sumA
            for lv in range(4):
                w = 1 << lv
                if lv:
                    pool.wait_ge(pool_step, lv)
                so, do = (1 if lv == 2 else 0), (1 if lv in (1, 3) else 0)
                lo = 2 * w - 1
                nc.gpsimd.tensor_tensor(dst[:, lv - do:CC - do, lo:L], src[:, lv - so:CC - so, lo:L],
                                        src[:, lv - so:CC - so, lo - w:L - w], ALU.add).then_inc(pool_step, 1)
                src, dst = (sumA, sumB) if lv % 2 == 0 else (sumB, sumA)
            pool.wait_ge(pool_step, 4)
            for g, w in enumerate(POOL_WINDOWS):
                s = (sumA[:, g, META:L] if g % 2 == 0 else sumB[:, g - 1, META:L])
                nc.gpsimd.tensor_scalar(s, s, 1.0 / w, None, ALU.mult).then_inc(pool_step, 1)
            for g in range(CC):
                s = (sumA[:, g, META:L] if g % 2 == 0 else sumB[:, g - 1, META:L])
                pool.wait_ge(pool_step, 5 + g)
                nc.gpsimd.tensor_tensor(uT[:, g, META:L], s, uT[:, g, META:L], ALU.subtract).then_inc(pooled, 1)
            for m in range(KC):
                pool.wait_ge(proj_read, 12 + m + 1)
                pool.wait_ge(ya_ready, m + 1)
                nc.gpsimd.tensor_tensor(mix[:, m, :], mix[:, m, :], gasig[:, m % 4, :], ALU.mult
                                        ).then_inc(ya_gated, 1)

        @block.scalar
        def _(act):
            act.wait_ge(stage_clear, 1)
            for name in ON_ACT:
                r0, k, ap = rows[name]
                act.dma_start(stage[r0:r0 + k, 0, :], ap.rearrange("o (r c) -> (o r) c", c=P)).then_inc(stage_in, 16)

            def root(i, k, rows_=P):
                act.wait_ge(meaned, k)
                nc.scalar.activation(ss[0:rows_, i:i + 1], ss[0:rows_, i:i + 1], ACT.Sqrt).then_inc(rooted, 1)

            def square(i, k, src, scratch, rows_=P):
                if k > 1:
                    act.wait_ge(squared_act, k - 1)
                nc.scalar.activation(scratch, src, ACT.Square, accum_out=ss[0:rows_, i:i + 1]
                                     ).then_inc(squared_act, 1)

            act.wait_ge(consts_a, 2)
            nc.scalar.activation(spare[:, :], ones[:, 0:1], ACT.Sqrt).then_inc(table_in, 1)
            root(0, 1)
            act.wait_ge(meta_in, 16)
            square(TT, 1, meta, workf[0:META, :], META)
            root(1, 2)
            root(TT, 3, META)
            act.wait_ge(par_turned, 1)
            nc.scalar.activation(par[:, :, :], bank(2, 2, P), ACT.Copy).then_inc(par_ready, 1)
            act.wait_ge(par_ready, 1)
            for t in range(TT):
                act.wait_ge(x_turned, 2 * t + 2)
                for i in range(4):
                    nc.scalar.activation(xnT[:, 4 + i, META + t * P:META + (t + 1) * P],
                                         ps[:, 4 + 2 * t + 1, i * P:(i + 1) * P], ACT.Copy, scale=col("g_mix", 4 + i)
                                         ).then_inc(xnT_act, 1)

            def evacuate(n, dst, func, name, m, w=SEQ):
                act.wait_ge(proj_done, n + 1)
                nc.scalar.activation(dst, ps[:, n % 4, 0:w], func, bias=col("b_in", m)).then_inc(proj_read, 1)

            act.wait_ge(par_ready, 1)
            for c in range(CC):
                evacuate(c, glu[:, c, PAD:LP], ACT.Identity, "b_in", CC + c, L)
            act.wait_ge(squared_act, 1)
            for c in range(CC):
                if c == 3:
                    act.wait_ge(glu_ready, 1)
                evacuate(4 + c, gtsig[:, c % 3, :], ACT.Sigmoid, "b_in", 2 * CC + c, L)
            for c in range(CC):
                evacuate(8 + c, uT[:, c, :], ACT.Identity, "b_in", c, L)
            for m in range(4):
                evacuate(12 + m, gasig[:, m, :], ACT.Sigmoid, "b_in", 3 * CC + m)
            for m in range(KC):
                act.wait_ge(pool_done, 2 * (m // 2) + 2)
                nc.scalar.activation(mix[:, m, :], ps[:, 4 + m // 2, (m % 2) * SEQ:(m % 2 + 1) * SEQ], ACT.Copy,
                                     scale=col("scale", m)).then_inc(ya_ready, 1)
            for m in range(4, KC):
                act.wait_ge(ya_gated, m - 3)
                evacuate(12 + m, gasig[:, m % 4, :], ACT.Sigmoid, "b_in", 3 * CC + m)
            for m in range(KC):
                evacuate(20 + m, gbsig[:, m, :], ACT.Sigmoid, "b_in", 3 * CC + KC + m)
                if m == 0:
                    act.wait_ge(centred, 1)
                    act.wait_ge(pooled, 4)
                    nc.scalar.activation(sq, conv, ACT.Square).then_inc(ln_squared, 1)
                if m == 2:
                    act.wait_ge(var_ready, 1)
                    nc.scalar.activation(lnr, lnr, ACT.Sqrt).then_inc(dev_ready, 1)
                if m == 4:
                    act.wait_ge(normed, 1)
                    for c in range(CC):
                        nc.scalar.activation(conv[:, c, :], conv[:, c, :], ACT.Identity, bias=col("ln_b", c),
                                             scale=col("ln_g", c)).then_inc(affine_done, 1)
                    act.wait_ge(affine_done, CC)
                    nc.scalar.activation(cvsig, conv, ACT.Sigmoid).then_inc(cvsig_ready, 1)

            for t in range(TT):
                root(3 + t, TT + 2 + t)
                act.wait_ge(inverted, TT + 2 + t)
                nc.scalar.activation(hs[:, t, :], h[:, t, :], ACT.Copy, scale=rstd[:, 3 + t:4 + t]
                                     ).then_inc(hs_ready, 1)
            for t in range(TT):
                act.wait_ge(negmax_ready, t + 1)
                nc.scalar.activation(expl[:, t, :], logits[:, t, :], ACT.Exp, bias=negmax[:, t:t + 1]
                                     ).then_inc(exp_ready, 1)

            def step(n):
                act.wait_ge(turned, n + 1)
                nc.scalar.activation(spread[:, :, :], bank(6, 2, SEQ), ACT.Copy).then_inc(spread_ready, 1)
                for i in range(2):
                    act.wait_ge(clamped, 4 * n + 2 * i + 1)
                    nc.scalar.activation(sig[:, :], work[:, 0, :], ACT.Sigmoid, scale=SWIGLU_ALPHA
                                         ).then_inc(sig_ready, 1)
                    act.wait_ge(act_turned, 2 * n + i + 1)
                    nc.scalar.activation(actT[:, i, :, :], bank(4 + i, FC // 2, P), ACT.Copy).then_inc(actT_ready, 1)
                for i in range(2):
                    act.wait_ge(dn_used, 8 * n + 4 * (i + 1))
                    nc.scalar.activation(acts[:, i, :], ps[:, 6 + i, :], ACT.Copy).then_inc(y_ready, 1)

            with act.Fori(0, PAIRS) as n:
                step(n)
            act.wait_ge(h_added, 4 * PAIRS + 4)
            act.wait_ge(flag_ready, 1)
            over = act.value_load(flag[0:1, 0:1], min_val=0, max_val=1)
            with act.If(over):
                with act.Fori(PAIRS, STEPS) as n:
                    step(n)
                act.wait_ge(h_added, 4 * STEPS + 4)

            root(5, 2 * TT + 2)
            square(6, 2, h[:, 1, :], gu_ring[:, 4, 0:D])
            root(6, 2 * TT + 3)

        @block.vector
        def _(dve):
            nc.vector.memset(stage, 0.0).then_inc(stage_clear, 1)
            nc.vector.memset(glu[:, :, 0:PAD], 0.0).then_inc(pads_made, 1)

            def square(i, k, src, scratch):
                if k > 1:
                    dve.wait_ge(squared, k - 1)
                nc.vector.scalar_tensor_tensor(scratch, src, 1.0, src, ALU.mult, ALU.mult,
                                               accum_out=ss[:, i:i + 1]).then_inc(squared, 1)
                dve.wait_ge(squared, k)

            def mean(i, rows_=P):
                nc.vector.tensor_scalar(ss[0:rows_, i:i + 1], ss[0:rows_, i:i + 1], 1.0 / D, RMS_EPS, ALU.mult,
                                        ALU.add).then_inc(meaned, 1)

            def invert(i, k, rows_=P):
                dve.wait_ge(rooted, k)
                nc.vector.reciprocal(rstd[0:rows_, i:i + 1], ss[0:rows_, i:i + 1]).then_inc(inverted, 1)
                dve.wait_ge(inverted, k)

            def norm_in(i, k, src, dst, rows_=P):
                invert(i, k, rows_)
                nc.vector.tensor_scalar(dst, src, rstd[0:rows_, i:i + 1], None, ALU.mult).then_inc(scaled, 1)

            dve.wait_ge(x_in[0], 16)
            square(0, 1, h[:, 0, :], junk)
            mean(0)
            dve.wait_ge(x_in[1], 16)
            square(1, 2, h[:, 1, :], junk)
            mean(1)
            norm_in(0, 1, h[:, 0, :], hs[:, 0, :])
            norm_in(1, 2, h[:, 1, :], hs[:, 1, :])
            dve.wait_ge(squared_act, 1)
            mean(TT, META)
            norm_in(TT, 3, meta, meta, META)
            dve.wait_ge(par_ready, 1)
            for t in range(TT):
                dve.wait_ge(x_turned, 2 * t + 1)
                nc.vector.tensor_tensor(xnT[:, 0:4, META + t * P:META + (t + 1) * P], bank(4 + 2 * t, 4, P),
                                        wide(col("g_mix", 0, 4), 4, P), ALU.mult).then_inc(xnT_ready, 1)
            dve.wait_ge(x_turned, 2 * TT + 1)
            nc.vector.tensor_tensor(xnT[:, :, 0:META], bank(0, KC, META), wide(col("g_mix", 0, KC), KC, META),
                                    ALU.mult).then_inc(xnT_ready, 1)

            for c in range(CC):
                dve.wait_ge(proj_read, 4 + c + 1)
                nc.vector.tensor_tensor(glu[:, c, PAD:LP], glu[:, c, PAD:LP], gtsig[:, c % 3, :], ALU.mult
                                        ).then_inc(glu_ready, 1)
            dve.wait_ge(pads_made, 1)
            dve.wait_ge(glu_ready, 4)
            for k in range(TAPS):
                for c in range(CC):
                    if k == 0:
                        ins = nc.vector.tensor_scalar(conv[:, c, :], glu[:, c, 0:SEQ], tap(0, c), col("b_dw", c),
                                                      ALU.mult, ALU.add)
                    else:
                        dve.wait_ge(conv_step, CC * (k - 1) + c + 1)
                        ins = nc.vector.scalar_tensor_tensor(conv[:, c, :], glu[:, c, k:k + SEQ], tap(k, c),
                                                             conv[:, c, :], ALU.mult, ALU.add)
                    ins.then_inc(conv_step, 1)
            dve.wait_ge(ln_summed, 1)
            nc.vector.scalar_tensor_tensor(conv, ps[:, 4, 0:SEQ].unsqueeze(1).to_broadcast([P, CC, SEQ]), -1.0 / CW,
                                           conv, ALU.mult, ALU.add).then_inc(centred, 1)
            dve.wait_ge(var_summed, 1)
            nc.vector.tensor_scalar(lnr, ps[:, 5, 0:SEQ], 1.0 / CW, LN_EPS, ALU.mult, ALU.add
                                    ).then_inc(var_ready, 1)
            dve.wait_ge(dev_ready, 1)
            nc.vector.reciprocal(lnr, lnr).then_inc(lnr_ready, 1)
            dve.wait_ge(lnr_ready, 1)
            nc.vector.tensor_tensor(conv, conv, lnr.unsqueeze(1).to_broadcast([P, CC, SEQ]), ALU.mult
                                    ).then_inc(normed, 1)
            dve.wait_ge(cvsig_ready, 1)
            nc.vector.tensor_tensor(conv, conv, cvsig, ALU.mult).then_inc(silu_ready, 1)
            dve.wait_ge(proj_read, NP)
            dve.wait_ge(ya_gated, KC)
            for q in range(KC // 2):
                dve.wait_ge(pw2_done, q + 1)
                for m in (2 * q, 2 * q + 1):
                    nc.vector.scalar_tensor_tensor(gbsig[:, m, :], ps[:, 4 + q, (m % 2) * SEQ:(m % 2 + 1) * SEQ],
                                                   col("b_pw2", m), gbsig[:, m, :], ALU.add, ALU.mult
                                                   ).then_inc(yb_gated, 1)
                dve.wait_ge(yb_gated, 2 * q + 2)
                nc.vector.tensor_tensor(mix[:, 2 * q:2 * q + 2, :], mix[:, 2 * q:2 * q + 2, :],
                                        gbsig[:, 2 * q:2 * q + 2, :], ALU.add).then_inc(mix_ready, 1)
            def turn_gain(t):
                for hf in range(2):
                    dve.wait_ge(hs_turned, 2 * t + hf + 1)
                    nc.vector.tensor_tensor(hT[:, 4 * hf:4 * hf + 4, t * P:(t + 1) * P], bank(4 + 2 * t + hf, 4, P),
                                            wide(col("g_ffn", 4 * hf, 4), 4, P), ALU.mult).then_inc(hT_ready, 1)

            def norm_ffn(t):
                dve.wait_ge(h_added, 2 * t + 2)
                square(3 + t, 3 + t, h[:, t, :], junk_ffn)
                mean(3 + t)
                invert(3 + t, TT + 2 + t)

            for t in range(TT):
                for hf in range(2):
                    dve.wait_ge(wout_done, 2 * t + hf + 1)
                    nc.vector.tensor_tensor(h[:, t, hf * 512:(hf + 1) * 512], h[:, t, hf * 512:(hf + 1) * 512],
                                            ps[:, 2 * t + hf, :], ALU.add).then_inc(h_added, 1)
                if t == 0:
                    norm_ffn(0)
                    turn_gain(0)
            turn_gain(1)
            norm_ffn(1)
            dve.wait_ge(logits_done, 1)
            nc.vector.tensor_copy(lgT, ps[:, 0, 0:SEQ]).then_inc(groups_ready, 1)
            dve.wait_ge(logits_turned, 1)
            nc.vector.tensor_reduce(logits, ps[:, 1, 0:TT * P].rearrange("p (t g e) -> p t e g", t=TT, g=4), AX_X,
                                    ALU.add).then_inc(logits_summed, 1)
            dve.wait_ge(logits_summed, 1)
            dve.wait_ge(router_in, 32)
            dve.wait_ge(consts_made, 5)
            for t in range(TT):
                nc.vector.scalar_tensor_tensor(logits[:, t, :], logits[:, t, :], rstd[:, 3 + t:4 + t], rb, ALU.mult,
                                               ALU.add).then_inc(logits_ready, 1)
            for t in range(TT):
                dve.wait_ge(logits_ready, t + 1)
                nc.vector.max(top[:, t, :], logits[:, t, :]).then_inc(top_ready, 1)
            for t in range(TT):
                dve.wait_ge(top_ready, t + 1)
                nc.vector.max_index(topi[:, t, :], top[:, t, :], logits[:, t, :]).then_inc(topi_ready, 1)
                nc.vector.tensor_scalar(negmax[:, t:t + 1], top[:, t, 0:1], -1.0, None, ALU.mult
                                        ).then_inc(negmax_ready, 1)
            for t in range(TT):
                dve.wait_ge(topi_ready, t + 1)
                nc.vector.tensor_copy(topf[:, t, :], topi[:, t, :]).then_inc(topf_ready, 1)
            for k in range(TOP_K):
                for t in range(TT):
                    if k == 0:
                        dve.wait_ge(topf_ready, t + 1)
                        ins = nc.vector.tensor_scalar(chosen[:, t, 0, :], expert_no[:, :], topf[:, t, 0:1], None,
                                                      ALU.is_equal)
                    else:
                        dve.wait_ge(chosen_step, TT * (k - 1) + t + 1)
                        ins = nc.vector.scalar_tensor_tensor(chosen[:, t, k, :], expert_no[:, :], topf[:, t, k:k + 1],
                                                             chosen[:, t, k - 1, :], ALU.is_equal, ALU.add)
                    ins.then_inc(chosen_step, 1)
            dve.wait_ge(chosen_step, TT * TOP_K)
            for t in range(TT):
                dve.wait_ge(exp_ready, t + 1)
                nc.vector.scalar_tensor_tensor(expl[:, t, :], expl[:, t, :], 1.0, chosen[:, t, TOP_K - 1, :],
                                               ALU.mult, ALU.mult, accum_out=esum[:, t:t + 1]).then_inc(esum_ready, 1)
            dve.wait_ge(esum_ready, TT)
            nc.vector.reciprocal(erec[:, :], esum[:, :]).then_inc(erec_ready, 1)
            dve.wait_ge(prefix_done, 1)
            for t in range(TT):
                nc.vector.scalar_tensor_tensor(place[:, t, 0:E], ps[:, 2, t * E:(t + 1) * E], 1.0,
                                               chosen[:, t, TOP_K - 1, :], ALU.add, ALU.mult).then_inc(place_ready, 1)
            dve.wait_ge(place_ready, TT)

            iota_pair = slot_no[:, 0:SLOTS].unsqueeze(1).unsqueeze(1).to_broadcast([P, TT, 2, SLOTS])
            iota_one = slot_no[:, :].unsqueeze(1).to_broadcast([P, TT, 2 * SLOTS])

            def select_pair(n, e, first=False):
                if not first:
                    dve.wait_ge(gathered, 2 * n)
                nc.vector.tensor_tensor(pick[:, :, :].rearrange("p t (i s) -> p t i s", i=2), iota_pair,
                                        place[:, :, bass.ds(e, 2)].unsqueeze(3).to_broadcast([P, TT, 2, SLOTS]),
                                        ALU.is_equal).then_inc(pick_made, 1)
                if first:
                    dve.wait_ge(erec_ready, 1)
                    for t in range(TT):
                        nc.vector.tensor_scalar(gates[:, t, 0:E], expl[:, t, :], erec[:, t:t + 1], None, ALU.mult
                                                ).then_inc(gates_ready, 1)
                    dve.wait_ge(gates_ready, TT)
                    dve.wait_ge(counts_done, 1)
                else:
                    dve.wait_ge(turned, n)
                dve.wait_ge(pick_made, n + 1)
                for t in range(TT):
                    nc.vector.tensor_tensor(
                        weigh[:, t, :, :, :],
                        pick[:, t, :].rearrange("p (i s) -> p i s", i=2).unsqueeze(2).to_broadcast([P, 2, 2, SLOTS]),
                        gates[:, t, bass.ds(e, 2)].unsqueeze(2).unsqueeze(3).to_broadcast([P, 2, 2, SLOTS]),
                        ALU.mult).then_inc(weigh_made, 1)

            def select_one(n, e):
                dve.wait_ge(gathered, 2 * n)
                nc.vector.tensor_tensor(pick[:, :, :], iota_one,
                                        place[:, :, bass.ds(e, 1)].to_broadcast([P, TT, 2 * SLOTS]),
                                        ALU.is_equal).then_inc(pick_made, 1)
                dve.wait_ge(turned, n)
                dve.wait_ge(pick_made, n + 1)
                for t in range(TT):
                    nc.vector.tensor_tensor(
                        weigh[:, t, :, :, :],
                        pick[:, t, :].rearrange("p (i s) -> p i s", i=2).unsqueeze(2).to_broadcast([P, 2, 2, SLOTS]),
                        gates[:, t, bass.ds(e, 1)].unsqueeze(2).unsqueeze(3).to_broadcast([P, 2, 2, SLOTS]),
                        ALU.mult).then_inc(weigh_made, 1)

            def gather_gain(n):
                for q in range(2):
                    dve.wait_ge(gathered, 2 * n + q + 1)
                    nc.vector.tensor_tensor(xg[:, 4 * q:4 * q + 4, :], bank(4 + q, 4, P),
                                            wide(col("g_ffn", 4 * q, 4), 4, P), ALU.mult).then_inc(xg_ready, 1)

            def swiglu(n, i):
                dve.wait_ge(gu_used, 16 * n + 8 * (i + 1))
                if i:
                    dve.wait_ge(act_ready, 2 * n + i)
                nc.vector.tensor_scalar(work[:, 0, :], ps[:, 2 * i, :], SWIGLU_LIMIT, None, ALU.min
                                        ).then_inc(clamped, 1)
                nc.vector.tensor_scalar(work[:, 1, :], ps[:, 2 * i + 1, :], SWIGLU_LIMIT, -SWIGLU_LIMIT, ALU.min,
                                        ALU.max).then_inc(clamped, 1)
                dve.wait_ge(sig_ready, 2 * n + i + 1)
                nc.vector.tensor_tensor(sig[:, :], work[:, 0, :], sig[:, :], ALU.mult).then_inc(gated, 1)
                dve.wait_ge(gated, 2 * n + i + 1)
                dve.wait_ge(clamped, 4 * n + 2 * i + 2)
                nc.vector.scalar_tensor_tensor(acts[:, i, :], work[:, 1, :], 1.0, sig[:, :], ALU.add, ALU.mult
                                               ).then_inc(act_ready, 1)

            def add_outputs(n):
                for q in range(4):
                    t, hf = q // 2, q % 2
                    dve.wait_ge(scattered, 4 * n + q + 1)
                    if q == 0:
                        dve.wait_ge(h_added, 4 * n + 4)
                    nc.vector.tensor_tensor(h[:, t, hf * 512:(hf + 1) * 512], h[:, t, hf * 512:(hf + 1) * 512],
                                            ps[:, q, :], ALU.add).then_inc(h_added, 1)

            select_pair(0, 0, first=True)
            dve.wait_ge(counts_done, 1)
            nc.vector.reduce_max(most[:, :], ps[0:1, 3, 0:E], AX_X).then_inc(most_ready, 1)
            dve.wait_ge(most_ready, 1)
            nc.vector.tensor_scalar(flag[:, :], most[:, :], float(SLOTS), None, ALU.is_gt).then_inc(flag_ready, 1)
            dve.wait_ge(flag_ready, 1)
            over = dve.value_load(flag[0:1, 0:1], min_val=0, max_val=1)
            with dve.Fori(0, PAIRS - 1) as n:
                gather_gain(n)
                swiglu(n, 0)
                select_pair(n + 1, 2 * n + 2)
                swiglu(n, 1)
                add_outputs(n)
            gather_gain(PAIRS - 1)
            swiglu(PAIRS - 1, 0)
            swiglu(PAIRS - 1, 1)
            add_outputs(PAIRS - 1)
            dve.wait_ge(h_added, 4 * PAIRS + 4)
            with dve.If(over):
                for r in range(2):
                    nc.vector.tensor_scalar(place[:, :, :], place[:, :, :], -float(SLOTS * (r + 1)), None, ALU.add
                                            ).then_inc(place_moved, 1)
                    dve.wait_ge(place_moved, r + 1)
                    with dve.Fori(0, E) as e:
                        n = PAIRS + r * E + e
                        select_one(n, e)
                        gather_gain(n)
                        swiglu(n, 0)
                        swiglu(n, 1)
                        add_outputs(n)
                dve.wait_ge(h_added, 4 * STEPS + 4)

            square(5, 5, h[:, 0, :], gu_ring[:, 3, 0:D])
            mean(5)
            dve.wait_ge(gfin_in, 16)
            for t in range(TT):
                invert(5 + t, 2 * TT + 2 + t)
                for hf in range(2):
                    cols = slice(hf * 512, (hf + 1) * 512)
                    nc.vector.scalar_tensor_tensor(outb[:, t, cols], h[:, t, cols], rstd[:, 5 + t:6 + t],
                                                   gfin[:, cols], ALU.mult, ALU.mult).then_inc(out_ready, 1)
                    if t == 0 and hf == 0:
                        dve.wait_ge(squared_act, 2)
                        mean(6)

        @block.tensor
        def _(pe):
            mm = nc.tensor.matmul
            def stay_awake(count, src):
                for _ in range(count):
                    mm(ps[:, 3, 0:P], src, src, start=True, stop=True)

            pe.wait_ge(consts_a, 2)
            stay_awake(14, ones)
            pe.wait_ge(consts_made, 1)
            for q in range(2 * TT):
                pe.wait_ge(scaled, q // 2 + 1)
                if q == 2:
                    pe.wait_ge(stage_in, 16 * (len(rows) + 1))
                    for i in range(2):
                        ins = nc.tensor.transpose(ps[:, 2, i * P:(i + 1) * P], stage[:, i, :], ident[:])
                    ins.then_inc(par_turned, 1)
                for i in range(4):
                    c = 4 * (q % 2) + i
                    ins = nc.tensor.transpose(ps[:, 4 + q, i * P:(i + 1) * P], hs[:, q // 2, c * P:(c + 1) * P],
                                              ident[:])
                ins.then_inc(x_turned, 1)
            pe.wait_ge(scaled, TT + 1)
            for c in range(KC):
                ins = nc.tensor.transpose(ps[:, 0, c * META:(c + 1) * META], meta[:, c * P:(c + 1) * P],
                                          ident[0:META, 0:META])
            ins.then_inc(x_turned, 1)

            pe.wait_ge(xnT_ready, TT + 1)
            pe.wait_ge(xnT_act, 4 * TT)

            def project(n):
                i, q = n // 4, n % 4
                if n in (0, 2):
                    pe.wait_ge(win_in[n // 2], 16)
                elif n % 4 == 0:
                    pe.wait_ge(win_in[i + 1], 16)
                if n >= 4:
                    pe.wait_ge(proj_read, n - 3)
                lo = 0 if n < 12 else META
                for k in range(KC):
                    ins = mm(ps[:, q, 0:L - lo], win_block(i)[:, k, q * P:(q + 1) * P], xnT[:, k, lo:L],
                             start=k == 0, stop=k == KC - 1)
                ins.then_inc(proj_done, 1)

            for n in range(16):
                project(n)
            pe.wait_ge(wpool_in, 16)
            for m in range(KC):
                g = m // 2
                pe.wait_ge(pooled, g + 1)
                mm(ps[:, 4 + m // 2, (m % 2) * SEQ:(m % 2 + 1) * SEQ], wpool[:, g, (m % 2) * P:(m % 2 + 1) * P],
                   uT[:, g, META:L], start=True, stop=True).then_inc(pool_done, 1)
            for n in range(16, 21):
                project(n)
            pe.wait_ge(consts_made, 4)
            pe.wait_ge(ya_ready, KC)
            for c in range(CC):
                pe.wait_ge(conv_step, CC * (TAPS - 1) + c + 1)
                ins = mm(ps[:, 4, 0:SEQ], ones[:], conv[:, c, :], start=c == 0, stop=c == CC - 1)
            ins.then_inc(ln_summed, 1)
            for n in range(21, 22):
                project(n)
            pe.wait_ge(ln_squared, 1)
            for c in range(CC):
                ins = mm(ps[:, 5, 0:SEQ], ones[:], sq[:, c, :], start=c == 0, stop=c == CC - 1)
            ins.then_inc(var_summed, 1)
            for n in range(22, NP):
                project(n)
            pe.wait_ge(pw2_in, 16)
            pe.wait_ge(silu_ready, 1)
            for m in range(KC):
                for c in range(CC):
                    ins = mm(ps[:, 4 + m // 2, (m % 2) * SEQ:(m % 2 + 1) * SEQ], pw2_sb[:, c, m * P:(m + 1) * P],
                             conv[:, c, :], start=c == 0, stop=c == CC - 1)
                if m % 2:
                    ins.then_inc(pw2_done, 1)
            pe.wait_ge(wout_in, 16)
            pe.wait_ge(proj_read, NP)
            for t in range(TT):
                for m in range(KC):
                    if t == 0:
                        pe.wait_ge(mix_ready, m // 2 + 1)
                    for hf in range(2):
                        ins = mm(ps[:, 2 * t + hf, :], mix[:, m, t * P:(t + 1) * P],
                                 wout_sb[:, m, hf * 512:(hf + 1) * 512], start=m == 0, stop=m == KC - 1)
                        if m == KC - 1:
                            ins.then_inc(wout_done, 1)
            for q in range(2 * TT):
                pe.wait_ge(h_added, q + 1)
                for i in range(4):
                    c = 4 * (q % 2) + i
                    ins = nc.tensor.transpose(ps[:, 4 + q, i * P:(i + 1) * P], h[:, q // 2, c * P:(c + 1) * P],
                                              ident[:])
                ins.then_inc(hs_turned, 1)
            pe.wait_ge(router_in, 32)
            for k in range(KC):
                g = k % 4
                if g == 0:
                    pe.wait_ge(hT_ready, 2 * TT - 1 + k // 4)
                ins = mm(ps[g * E:(g + 1) * E, 0, 0:SEQ], rw[:, k, :], hT[:, k, :], start=k < 4, stop=k >= 4)
            ins.then_inc(logits_done, 1)
            pe.wait_ge(groups_ready, 1)
            for t in range(TT):
                ins = nc.tensor.transpose(ps[:, 1, t * P:(t + 1) * P], lgT[:, t * P:(t + 1) * P], ident[:])
            ins.then_inc(logits_turned, 1)
            stay_awake(8, ident[:])
            pe.wait_ge(chosen_step, TT * TOP_K)
            last = chosen[:, :, TOP_K - 1, :]
            mm(ps[:, 2, 0:TT * E], earlier, last, start=True, stop=True)
            mm(ps[:, 2, E:TT * E], ones, last[:, 0, :], start=False, stop=True, skip_group_check=True
               ).then_inc(prefix_done, 1)
            stay_awake(4, ident[:])
            for t in range(TT):
                ins = mm(ps[:, 3, 0:E], ones, last[:, t, :], start=t == 0, stop=t == TT - 1)
            ins.then_inc(counts_done, 1)

            def step(n):
                pe.wait_ge(pick_made, n + 1)
                for c in range(KC):
                    for t in range(TT):
                        ins = mm(ps[:, 4 + c // 4, (c % 4) * P:(c % 4 + 1) * P], hs[:, t, c * P:(c + 1) * P],
                                 pick[:, t, :], start=t == 0, stop=t == TT - 1)
                    if c % 4 == 3:
                        ins.then_inc(gathered, 1)
                def turn_weights():
                    pe.wait_ge(weigh_made, 2 * n + 2)
                    for i in range(2):
                        for t in range(TT):
                            ins = nc.tensor.transpose(ps[:, 6, i * SEQ + t * P:i * SEQ + (t + 1) * P],
                                                      weigh[:, t, i, :, :].rearrange("p a b -> p (a b)"), ident[:])
                    ins.then_inc(turned, 1)

                def turn_acts(i):
                    pe.wait_ge(act_ready, 2 * n + i + 1)
                    for b in range(FC // 2):
                        ins = nc.tensor.transpose(ps[:, 4 + i, b * P:(b + 1) * P], acts[:, i, b * P:(b + 1) * P],
                                                  ident[:])
                    ins.then_inc(act_turned, 1)

                def scatter(i):
                    pe.wait_ge(y_ready, 2 * n + i + 1)
                    for t in range(TT):
                        for hf in range(2):
                            ins = mm(ps[:, 2 * t + hf, :], spread[hf * SLOTS:(hf + 1) * SLOTS, i, t * P:(t + 1) * P],
                                     acts[hf * SLOTS:(hf + 1) * SLOTS, i, :], start=i == 0, stop=i == 1)
                            if i == 1:
                                ins.then_inc(scattered, 1)

                pe.wait_ge(h_added, 4 * n + 4)
                pe.wait_ge(most_ready, 1)
                for i in range(2):
                    for k in range(KC):
                        if i == 0 and k % 4 == 0:
                            pe.wait_ge(xg_ready, 2 * n + k // 4 + 1)
                        if k == KC - 1:
                            pe.wait_ge(bias_in[i], 32 * n + 32)
                            for g in range(2):
                                for hf in range(2):
                                    mm(ps[hf * SLOTS:(hf + 1) * SLOTS, 2 * i + g, :], seg[:, 2 * g + hf, :],
                                       bias[:, i, :], start=False, stop=False)
                        pe.wait_ge(gu_in[i * KC + k], 16 * n + 16)
                        for g in range(2):
                            for hf in range(2):
                                ins = mm(ps[hf * SLOTS:(hf + 1) * SLOTS, 2 * i + g, :],
                                         xg[:, k, i * SLOTS:(i + 1) * SLOTS],
                                         gu_ring[:, i * KC + k, g * F + hf * 512:g * F + (hf + 1) * 512],
                                         start=k == 0, stop=k == KC - 1)
                        ins.then_inc(gu_used, 1)
                        if i == 0 and k == 3:
                            turn_weights()
                        if i == 1 and k == 3:
                            turn_acts(0)
                pe.wait_ge(spread_ready, n + 1)
                for i in range(2):
                    pe.wait_ge(actT_ready, 2 * n + i + 1)
                    for hf in range(2):
                        mm(ps[hf * SLOTS:(hf + 1) * SLOTS, 6 + i, :], seg[:, 4 + hf, :], bias[:, i, :],
                           start=True, stop=False)
                    if i == 1:
                        scatter(0)
                    for f in range(4):
                        pe.wait_ge(dn_in[f], 32 * n + 16 * (i + 1))
                        for j in range(2):
                            c = 2 * f + j
                            for hf in range(2):
                                ins = mm(ps[hf * SLOTS:(hf + 1) * SLOTS, 6 + i, :],
                                         actT[:, i, c % 4, (c // 4) * SLOTS:(c // 4 + 1) * SLOTS],
                                         dn_ring[:, f, j * D + hf * 512:j * D + (hf + 1) * 512],
                                         start=False, stop=c == FC - 1)
                        ins.then_inc(dn_used, 1)
                        if i == 0 and f == 2:
                            turn_acts(1)
                scatter(1)

            pe.wait_ge(hs_ready, TT)
            with pe.Fori(0, PAIRS) as n:
                step(n)
            pe.wait_ge(flag_ready, 1)
            over = pe.value_load(flag[0:1, 0:1], min_val=0, max_val=1)
            with pe.If(over):
                with pe.Fori(PAIRS, STEPS) as n:
                    step(n)


_INS = ["x", "meta_tokens", "norm_mix_g", "w_in", "b_in", "w_pool_grp", "pool_scale", "w_dwconv", "b_dwconv",
        "conv_ln_g", "conv_ln_b", "w_pw2", "b_pw2", "w_out", "norm_ffn_g", "router_w", "router_b", "w_gate_up",
        "b_gate_up", "w_down", "b_down", "norm_final_g"]


def kernel(**inputs):
    import numpy as _np
    import concourse.bacc as _bacc
    from concourse import mybir as _mybir
    from concourse.bass_utils import run_bass_kernel_spmd as _run

    nc = _bacc.Bacc("TRN2", target_bir_lowering=False, num_devices=1)
    arrays, args = {}, []
    for name in _INS:
        a = _np.ascontiguousarray(inputs[name])
        arrays[f"in_{name}"] = a
        args.append(nc.dram_tensor(f"in_{name}", a.shape, _mybir.dt.from_np(a.dtype), kind="ExternalInput").ap())
    args.append(nc.dram_tensor("out_0", inputs["x"].shape, _mybir.dt.float32, kind="ExternalOutput").ap())
    block_kernel(nc, *args)
    r = _run(nc, [arrays], core_ids=[0])
    return r.results[0]["out_0"]
```
